# Optimizing a Trainium2 kernel written in Bass

```python
import jax
import jax.numpy as jnp
from jax import lax
import numpy as np

'''Bidirectional hybrid encoder block (1 layer).

16 learned meta tokens are prepended to x (BATCH, SEQ, D_MODEL), giving L = SEQ + 16 positions.
Per layer: h += W_o( sigmoid(g_A) * mLSTM_bidir(RMSNorm(h)) + sigmoid(g_B) * ConformerConv(RMSNorm(h)) )
           h += PEER(RMSNorm(h))
The two token mixers read ONE combined input projection of the same RMSNorm output; its columns
are partitioned into mLSTM q/k/v/output-gate/input-gate/forget-gate (separate gates per direction),
the Conformer GLU pointwise channels, and the two per-channel branch gates.
Final RMSNorm, meta tokens dropped. Output: (BATCH, SEQ, D_MODEL).
'''

D_MODEL = 2048
BATCH = 1
SEQ = 512
DEPTH = 1

N_META = 16
CHUNK = 64
META_PAD = CHUNK - N_META
MLSTM_HEADS = 8
QK_HEAD_DIM = D_MODEL // 16
V_HEAD_DIM = D_MODEL // 8
D_QK = MLSTM_HEADS * QK_HEAD_DIM
D_V = MLSTM_HEADS * V_HEAD_DIM
D_CONV = D_MODEL
CONV_WIDTH = 31
PEER_HEADS = 8
PEER_KEYS = 128
PEER_EXPERTS = PEER_KEYS * PEER_KEYS
PEER_TOPK = 16
PEER_QDIM = 256
PEER_HALF = PEER_QDIM // 2
PEER_BLOCK = 128
FORGET_BIAS = 3.0
LOG_ZERO_GATE = -1.0e4
EPS = 1e-6
SEG_SIZES = (D_QK, D_QK, D_V, D_V, MLSTM_HEADS, MLSTM_HEADS, MLSTM_HEADS, MLSTM_HEADS, 2 * D_CONV, 2 * D_MODEL)
SPLIT_POINTS = tuple(sum(SEG_SIZES[:i + 1]) for i in range(len(SEG_SIZES) - 1))
D_IN_TOTAL = sum(SEG_SIZES)

kernel_name = 'hybrid_mlstm_conformer_peer_encoder'

def rmsnorm(x, w):
    xf = x.astype(jnp.float32)
    y = xf * lax.rsqrt(jnp.mean(xf * xf, axis=-1, keepdims=True) + EPS)
    return (y * w.astype(jnp.float32)).astype(x.dtype)

def layernorm(x, w, b):
    xf = x.astype(jnp.float32)
    xc = xf - jnp.mean(xf, axis=-1, keepdims=True)
    var = jnp.mean(xc * xc, axis=-1, keepdims=True)
    y = xc * lax.rsqrt(var + EPS) * w.astype(jnp.float32) + b.astype(jnp.float32)
    return y.astype(x.dtype)

def mlstm_chunkwise(q, k, v, log_i, log_f):
    B, H, P, dk = q.shape
    dv = v.shape[-1]
    n = P // CHUNK
    q = q.reshape(B, H, n, CHUNK, dk) * (dk ** -0.5)
    k = k.reshape(B, H, n, CHUNK, dk)
    v = v.reshape(B, H, n, CHUNK, dv)
    log_i = log_i.reshape(B, H, n, CHUNK)
    log_f = log_f.reshape(B, H, n, CHUNK)
    b = jnp.cumsum(log_f, axis=-1)
    g = b[..., -1]
    a = g[..., None] - b + log_i

    def step(carry, xs):
        C, nv, m = carry
        k_c, v_c, a_c, g_c = xs
        m_new = jnp.maximum(g_c + m, jnp.max(a_c, axis=-1))
        decay = jnp.exp(g_c + m - m_new)
        w = jnp.exp(a_c - m_new[..., None])
        C_new = decay[..., None, None] * C + jnp.einsum('bhs,bhsv,bhsd->bhvd', w, v_c, k_c)
        n_new = decay[..., None] * nv + jnp.einsum('bhs,bhsd->bhd', w, k_c)
        return (C_new, n_new, m_new), (C, nv, m)

    init = (jnp.zeros((B, H, dv, dk), jnp.float32), jnp.zeros((B, H, dk), jnp.float32),
            jnp.zeros((B, H), jnp.float32))
    xs = (jnp.moveaxis(k, 2, 0), jnp.moveaxis(v, 2, 0), jnp.moveaxis(a, 2, 0), jnp.moveaxis(g, 2, 0))
    _, (C_prev, n_prev, m_prev) = lax.scan(step, init, xs)
    C_prev = jnp.moveaxis(C_prev, 0, 2)
    n_prev = jnp.moveaxis(n_prev, 0, 2)
    m_prev = jnp.moveaxis(m_prev, 0, 2)

    inter = b + m_prev[..., None]
    lower = jnp.tril(jnp.ones((CHUNK, CHUNK), dtype=bool))
    intra = b[..., :, None] - b[..., None, :] + log_i[..., None, :]
    intra = jnp.where(lower, intra, -jnp.inf)
    m = jnp.maximum(inter, jnp.max(intra, axis=-1))
    S = jnp.einsum('bhncd,bhnsd->bhncs', q, k) * jnp.exp(intra - m[..., None])
    w_inter = jnp.exp(inter - m)
    num = jnp.einsum('bhncs,bhnsv->bhncv', S, v) + w_inter[..., None] * jnp.einsum('bhnvd,bhncd->bhncv', C_prev, q)
    den = jnp.sum(S, axis=-1) + w_inter * jnp.einsum('bhnd,bhncd->bhnc', n_prev, q)
    h = num / jnp.maximum(jnp.abs(den), jnp.exp(-m))[..., None]
    return h.reshape(B, H, P, dv)

def mlstm_branch(q, k, v, o, i_f, f_f, i_b, f_b, norm_w, w_out):
    B, L, _ = q.shape

    def heads(t, dh):
        t = t.astype(jnp.float32).reshape(B, L, MLSTM_HEADS, dh).transpose(0, 2, 1, 3)
        return jnp.pad(t, ((0, 0), (0, 0), (META_PAD, 0), (0, 0)))

    def gate(t, fill):
        t = t.astype(jnp.float32).transpose(0, 2, 1)
        return jnp.pad(t, ((0, 0), (0, 0), (META_PAD, 0)), constant_values=fill)

    qh = heads(q, QK_HEAD_DIM)
    kh = heads(k, QK_HEAD_DIM)
    vh = heads(v, V_HEAD_DIM)
    li_f = gate(i_f, LOG_ZERO_GATE)
    lf_f = gate(jax.nn.log_sigmoid(f_f.astype(jnp.float32)), 0.0)
    li_b = gate(i_b, LOG_ZERO_GATE)
    lf_b = gate(jax.nn.log_sigmoid(f_b.astype(jnp.float32)), 0.0)

    def flip(t):
        return jnp.flip(t, axis=2)

    h_fwd = mlstm_chunkwise(qh, kh, vh, li_f, lf_f)
    h_bwd = flip(mlstm_chunkwise(flip(qh), flip(kh), flip(vh), flip(li_b), flip(lf_b)))
    hs = (h_fwd + h_bwd)[:, :, META_PAD:]
    hs = hs * lax.rsqrt(jnp.mean(hs * hs, axis=-1, keepdims=True) + EPS)
    hs = hs.transpose(0, 2, 1, 3).reshape(B, L, D_V) * norm_w.astype(jnp.float32)
    hs = hs * jax.nn.sigmoid(o.astype(jnp.float32))
    return hs.astype(q.dtype) @ w_out

def conv_branch(glu, conv_w, conv_b, ln_w, ln_b, w_out, b_out):
    a, g = jnp.split(glu, 2, axis=-1)
    c = a * jax.nn.sigmoid(g)
    c = lax.conv_general_dilated(
        c, conv_w[:, None, :].astype(c.dtype), window_strides=(1,),
        padding=[(CONV_WIDTH // 2, CONV_WIDTH // 2)],
        dimension_numbers=('NWC', 'WIO', 'NWC'), feature_group_count=D_CONV) + conv_b
    c = jax.nn.silu(layernorm(c, ln_w, ln_b))
    return c @ w_out + b_out

def peer(u, w_q, sub_keys, expert_u, expert_v):
    B, L, D = u.shape
    T = B * L
    n_blk = -(-T // PEER_BLOCK)
    t = jnp.pad(u.reshape(T, D), ((0, n_blk * PEER_BLOCK - T), (0, 0))).reshape(n_blk, PEER_BLOCK, D)

    def block(tb):
        qry = (tb @ w_q).reshape(PEER_BLOCK, PEER_HEADS, 2, PEER_HALF)
        s = jnp.einsum('thpd,pkd->thpk', qry, sub_keys)
        sv, si = lax.top_k(s, PEER_TOPK)
        cand = (sv[:, :, 0, :, None] + sv[:, :, 1, None, :]).reshape(PEER_BLOCK, PEER_HEADS, PEER_TOPK * PEER_TOPK)
        cidx = (si[:, :, 0, :, None] * PEER_KEYS + si[:, :, 1, None, :]).reshape(PEER_BLOCK, PEER_HEADS, PEER_TOPK * PEER_TOPK)
        top, pos = lax.top_k(cand, PEER_TOPK)
        eidx = jnp.take_along_axis(cidx, pos, axis=-1)
        gates = jax.nn.softmax(top.astype(jnp.float32), axis=-1)
        z = jnp.einsum('thed,td->the', expert_u[eidx], tb)
        act = (gates * jax.nn.gelu(z.astype(jnp.float32))).astype(tb.dtype)
        return jnp.einsum('the,thed->td', act, expert_v[eidx])

    out = lax.map(block, t)
    return out.reshape(n_blk * PEER_BLOCK, D)[:T].reshape(B, L, D)

def hybrid_layer(h, norm1_w, w_in, b_in, mlstm_norm_w, w_mlstm_out, conv_w, conv_b, conv_ln_w, conv_ln_b,
                 w_conv_out, b_conv_out, w_o, norm2_w, peer_w_q, peer_sub_keys, peer_u, peer_v):
    u = rmsnorm(h, norm1_w)
    proj = u @ w_in + b_in
    q, k, v, o, i_f, f_f, i_b, f_b, glu, gates = jnp.split(proj, SPLIT_POINTS, axis=-1)
    y_a = mlstm_branch(q, k, v, o, i_f, f_f, i_b, f_b, mlstm_norm_w, w_mlstm_out)
    y_b = conv_branch(glu, conv_w, conv_b, conv_ln_w, conv_ln_b, w_conv_out, b_conv_out)
    g_a, g_b = jnp.split(gates, 2, axis=-1)
    merged = jax.nn.sigmoid(g_a) * y_a + jax.nn.sigmoid(g_b) * y_b
    h = h + merged @ w_o
    h = h + peer(rmsnorm(h, norm2_w), peer_w_q, peer_sub_keys, peer_u, peer_v)
    return h

def setup_inputs(seed: int = 0) -> dict:
    key = jax.random.key(seed)
    ks = jax.random.split(key, 20)

    def nrm(kk, shape, scale):
        return jax.random.normal(kk, shape, jnp.float32) * scale

    f_f0 = SPLIT_POINTS[4]
    f_b0 = SPLIT_POINTS[6]
    b_in = nrm(ks[4], (DEPTH, D_IN_TOTAL), 0.02)
    b_in = b_in.at[:, f_f0:f_f0 + MLSTM_HEADS].add(FORGET_BIAS).at[:, f_b0:f_b0 + MLSTM_HEADS].add(FORGET_BIAS)
    return {
        'x': nrm(ks[0], (BATCH, SEQ, D_MODEL), 1.0),
        'meta_tokens': nrm(ks[1], (N_META, D_MODEL), 1.0),
        'norm1_w': 1.0 + nrm(ks[2], (DEPTH, D_MODEL), 0.02),
        'w_in': nrm(ks[3], (DEPTH, D_MODEL, D_IN_TOTAL), D_MODEL ** -0.5),
        'b_in': b_in,
        'mlstm_norm_w': 1.0 + nrm(ks[5], (DEPTH, D_V), 0.02),
        'w_mlstm_out': nrm(ks[6], (DEPTH, D_V, D_MODEL), D_V ** -0.5),
        'conv_w': nrm(ks[7], (DEPTH, CONV_WIDTH, D_CONV), CONV_WIDTH ** -0.5),
        'conv_b': nrm(ks[8], (DEPTH, D_CONV), 0.02),
        'conv_ln_w': 1.0 + nrm(ks[9], (DEPTH, D_CONV), 0.02),
        'conv_ln_b': nrm(ks[10], (DEPTH, D_CONV), 0.02),
        'w_conv_out': nrm(ks[11], (DEPTH, D_CONV, D_MODEL), D_CONV ** -0.5),
        'b_conv_out': nrm(ks[12], (DEPTH, D_MODEL), 0.02),
        'w_o': nrm(ks[13], (DEPTH, D_MODEL, D_MODEL), D_MODEL ** -0.5),
        'norm2_w': 1.0 + nrm(ks[14], (DEPTH, D_MODEL), 0.02),
        'peer_w_q': nrm(ks[15], (DEPTH, D_MODEL, PEER_HEADS * PEER_QDIM), D_MODEL ** -0.5),
        'peer_sub_keys': nrm(ks[16], (DEPTH, 2, PEER_KEYS, PEER_HALF), PEER_HALF ** -0.5),
        'peer_u': nrm(ks[17], (DEPTH, PEER_EXPERTS, D_MODEL), D_MODEL ** -0.5),
        'peer_v': nrm(ks[18], (DEPTH, PEER_EXPERTS, D_MODEL), 0.5),
        'final_norm_w': 1.0 + nrm(ks[19], (D_MODEL,), 0.02),
    }

def reference(x, meta_tokens, norm1_w, w_in, b_in, mlstm_norm_w, w_mlstm_out, conv_w, conv_b, conv_ln_w,
              conv_ln_b, w_conv_out, b_conv_out, w_o, norm2_w, peer_w_q, peer_sub_keys, peer_u, peer_v,
              final_norm_w):
    B = x.shape[0]
    meta = jnp.broadcast_to(meta_tokens[None].astype(x.dtype), (B, N_META, x.shape[-1]))
    h = jnp.concatenate([meta, x], axis=1)
    for layer in range(DEPTH):
        h = hybrid_layer(h, norm1_w[layer], w_in[layer], b_in[layer], mlstm_norm_w[layer], w_mlstm_out[layer],
                         conv_w[layer], conv_b[layer], conv_ln_w[layer], conv_ln_b[layer], w_conv_out[layer],
                         b_conv_out[layer], w_o[layer], norm2_w[layer], peer_w_q[layer], peer_sub_keys[layer],
                         peer_u[layer], peer_v[layer])
    h = rmsnorm(h, final_norm_w)
    return h[:, N_META:]


_drawn_inputs = setup_inputs


def setup_inputs(seed=0):
    import zlib

    import numpy as np

    out = dict(_drawn_inputs(seed))
    spreads = {}
    factors = {}
    for name, (base, spread) in spreads.items():
        noise = np.random.default_rng([zlib.crc32(name.encode()), seed]).standard_normal(out[name].shape)
        drawn = base * np.exp(spread * noise) if base else spread * noise
        out[name] = jnp.asarray(drawn.astype(out[name].dtype))
    for name, factor in factors.items():
        out[name] = (out[name] * factor).astype(out[name].dtype)
    return out
```

```python
from contextlib import ExitStack

import numpy as np

import concourse.bass as bass
from concourse import mybir

F32 = mybir.dt.float32
F32R = mybir.dt.float32r
U32 = mybir.dt.uint32
ALU = mybir.AluOpType
ACT = mybir.ActivationFunctionType
AX = mybir.AxisListType
ds = bass.ds

P = 128
D = 2048
KT = D // P
NM = 16
T = 512
L = T + NM
HALF = L // 2
TT = T // P
NH = 8
CW = 31
KEYS = 128
PH = 8
TOPK = 16
QSCALE = float(P) ** -0.5
EPS = 1e-6
NEG = -3.0e38

NB_A1, NB_A2, NB_16, NB_E = 6 * NH, 4 * KT, 16, 128
A1, A2 = 0, NB_A1
B1 = A2 + NB_A2
B2 = B1 + NB_16
C1 = B2 + NB_16
Q1 = C1 + NB_16
Z1 = Q1 + NB_16
O1 = Z1 + NB_E
END = O1 + NB_E
Z_LOOK, Z_GATE = 16, 64
TOK = T // Z_GATE
CH = 64
GJ = 8

F_OFF = [0, 512, 896, 1152]
B_OFF = [0, 128, 384, 768]
P_W = 1280


def encoder_block(nc, xT, w_proj, w_gate, b_gate, w_mo, w_co, w_o, w_q, u_blocks, v_blocks, cols,
                  bias_proj, conv_w, sub_keys, out):
    rows_dram = nc.dram_tensor("rows_scratch", (NH, 4, T), F32, kind="Internal").ap()
    ga_dram = nc.dram_tensor("gate_a_scratch", (KT, P, T), F32, kind="Internal").ap()
    gb_dram = nc.dram_tensor("gate_b_scratch", (KT, P, T), F32, kind="Internal").ap()
    h_dram = nc.dram_tensor("h_scratch", (P, KT * T), F32, kind="Internal").ap()
    z_dram = nc.dram_tensor("z_scratch", (NB_E, P, T), F32, kind="Internal").ap()
    g_dram = nc.dram_tensor("g_scratch", (T // CH, P, KEYS * CH), F32, kind="Internal").ap()

    at = [(nc.sbuf_base + 31) // 32 * 32]

    def place(name, shape, dt, offset=None):
        size = 4 * int(np.prod(shape[1:]))
        where = at[0] if offset is None else offset
        t = nc.alloc_sbuf_tensor_at(name, shape, dt, offset=where)
        if offset is None:
            at[0] += (size + 31) // 32 * 32
        return t

    XH = place("x_hi", [P, KT, L], F32R)
    XL = place("x_lo", [P, KT, L], F32R)
    RAW = [place(f"w_raw{s}", [P, D], F32) for s in range(2)]
    WH = [place(f"w_hi{s}", [P, D], F32R) for s in range(2)]
    WL = [place(f"w_lo{s}", [P, D], F32R) for s in range(2)]
    col = place("columns", [P, 9, KT], F32)
    N1W, N2W, FNW, MNW, CB, LNW, LNB, BCO, EPSC = range(9)
    bias = place("bias_proj", [P, NB_A1 + NB_A2], F32)
    nbias = place("neg_bias_o", [P, NB_A1], F32)
    cw = place("conv_w", [P, KT * CW], F32)
    sk = place("sub_keys", [P, 2, KEYS], F32)
    ones = place("ones", [P, P], F32)
    zer = place("zeros", [P, P], F32)
    ident = place("ident", [P, P], F32)
    iota = place("iota", [P, P], F32)
    cT = place("c_cols", [P, 2, TT, NH], F32)
    cM = place("c_meta", [NM, NH], F32)
    r1 = at[0]
    R1 = place("r1", [P, KT, L], F32)
    r2 = at[0]
    R2 = place("r2", [P, KT, T], F32)
    dd = at[0]
    assert nc.sbuf_usable_end - dd >= 35000, nc.sbuf_usable_end - dd

    def lay(start, items):
        made, where = [], start
        for name, shape, dt in items:
            made.append(place(name, shape, dt, where))
            where += (4 * int(np.prod(shape[1:])) + 31) // 32 * 32
        return made, where

    (sq0, sq1, rb1, wg, bg, gsb), e = lay(dd, [("sq0", [P, L], F32), ("sq1", [P, L], F32), ("rb1", [P, L], F32),
                                          ("w_gate", [P, KT, 32], F32), ("b_gate", [32, 1], F32), ("gate_rows", [32, L], F32)])
    (gi, gf, gt, gF, gM, gz), e2 = lay(r2, [(n, [NH, 2, L], F32) for n in ("log_i", "f_pre", "g_tmp", "cum_f", "cum_max")]
                                  + [("g_zero", [NH, L], F32)])
    assert e2 <= dd
    (kT, qT, vT, V, VM, PF, PB, PM), e3 = lay(r1, [("kT", [P, L], F32), ("qT", [P, T], F32), ("vT", [P, 2, L], F32),
        ("V", [P, TT, 2 * P], F32), ("V_meta", [NM, 2 * P], F32), ("P_fwd", [P, P_W], F32), ("P_bwd", [P, P_W], F32),
        ("P_meta", [NM, T], F32)])
    assert e3 <= r2
    (rows, og, dF, dB, hh, hb), e4 = lay(dd, [("rows", [P, 4, T], F32), ("o_gate", [P, 2, T], F32), ("den_f", [P, T], F32),
        ("den_b", [P, T], F32), ("h_head", [P, 2, T], F32), ("h_back", [P, 2, T], F32)])
    (hs_sq, rs_h), e4 = lay(e4, [("h_sq", [P, 2, T], F32), ("rstd_h", [P, T], F32)])
    (cb, sg, st0, st1), e5 = lay(dd, [("glu", [P, 544], F32), ("glu_sig", [P, L], F32), ("ga_stage", [P, T], F32),
                                  ("gb_stage", [P, T], F32)])
    (side0, side1, sqa, sqb, sqc, sqd, rsB, tmpB), e6 = lay(e5, [(n, [P, T], F32) for n in
        ("side0", "side1", "sqa", "sqb", "sqc", "sqd", "rstd_b", "tmp_b")])
    SQ = [sqa, sqb, sqc, sqd]
    side = [side0, side1]
    (qr0, qr1), e7 = lay(e6, [("qry0", [P, T], F32), ("qry1", [P, T], F32)])
    qry = [qr0, qr1]
    (SIF, S2, CD, C2, TV, TP, TA, TB, SV0, SV1, SI0, SI1, CV, CI, CU), e8 = lay(r2, [("si_f", [P, TT, 2 * PH, TOPK], F32),
        ("s_rest", [P, TT, KEYS], F32), ("cand", [P, TT, 256], F32), ("cand_rest", [P, TT, 256], F32),
        ("top_v", [P, TT, PH, TOPK], F32), ("top_pos", [P, TT, PH, TOPK], U32), ("top_a", [P, TT, PH * TOPK], F32),
        ("top_b", [P, TT, PH * TOPK], F32), ("sv0", [P, TT, TOPK], F32), ("sv1", [P, TT, TOPK], F32),
        ("si0", [P, TT, TOPK], U32), ("si1", [P, TT, TOPK], U32), ("cand_v", [P, TT, TOPK], F32),
        ("cand_pos", [P, TT, TOPK], U32), ("pos_bits", [P, TT, PH, TOPK], U32)])
    assert e8 <= dd, (e8, dd)
    (EQ, GA, EI, EJ), e9 = lay(dd + 4096, [("eq", [P, P * TOPK], F32), ("ga", [P, TT, PH * TOPK], F32),
                                   ("ei", [P, TT, P], F32), ("ej", [P, TT, P], F32)])
    smx = place("smx", [P, TT * PH], F32, e9)
    e9 += 128
    (zs0, zs1, IT, JT, AH, AL), e10 = lay(dd, [("z_stage0", [P, T], F32), ("z_stage1", [P, T], F32), ("i_t", [P, T], F32),
        ("j_t", [P, T], F32), ("a_hi", [P, T], F32R), ("a_lo", [P, T], F32R)])
    zs = [zs0, zs1]
    hot, e11 = lay(e10, [(f"{n}{s}", [P, 4, P], F32R) for s in range(2) for n in ("hot_i", "hot_jh", "hot_jl")])
    (GB0, GB1), e12 = lay(r1, [("g_chunk0", [P, KEYS * CH], F32), ("g_chunk1", [P, KEYS * CH], F32)])
    GB = [GB0, GB1]
    assert e12 <= dd
    (GG0, GG1), e13 = lay(r1, [(f"g_group{s}", [P, T // CH, GJ * CH], F32) for s in range(2)])
    assert e13 <= r2
    (ZG1,), e14 = lay(dd, [("z_group1", [P, GJ, T], F32)])
    (ZG0,), e14 = lay(e14 + 2048, [("z_group0", [P, GJ, T], F32)])
    GG, ZG = [GG0, GG1], [ZG0, ZG1]
    for end in (e, e4, e5, e6, e7, e9, e11, e14):
        assert end <= nc.sbuf_usable_end, (end - dd, nc.sbuf_usable_end - dd)

    with ExitStack() as ctx:
        bk = [ctx.enter_context(nc.psum_tensor(f"bank{i}", [P, 512], F32)) for i in range(8)]
        A = bk[3:]

        def sem(name):
            return ctx.enter_context(nc.semaphore(name))

        w_loaded = [sem("w_loaded0"), sem("w_loaded1")]
        w_hi = sem("w_hi")
        w_lo = sem("w_lo")
        w_used = sem("w_used")
        evac_v = sem("evac_v")
        evac_a = sem("evac_a")
        x_hi = sem("x_hi_done")
        x_lo = sem("x_lo_done")
        v_step = sem("v_step")
        const_ld = sem("const_loaded")
        x_ld = [sem(f"x_loaded{i}") for i in range(4)]
        pool_const = sem("pool_const")
        sq_rdy, ss_use = sem("square_ready"), sem("square_used")
        ss_rdy = sem("sum_ready")
        rt_rdy = sem("root_ready")
        u_rdy = sem("u_ready")
        g_rdy, g_row, g_split = sem("gates_ready"), sem("gate_rows_ready"), sem("gate_rows_split")
        ga_step = sem("gate_act")
        gv = sem("gate_vec")
        c_rdy = sem("c_transposed")
        c_ev = sem("c_columns_ready")
        r_st = sem("rows_stored")
        r_ld = sem("rows_loaded")
        e_rdy, e_exp, e_msk = sem("exponent_ready"), sem("exp_ready"), sem("mask_done")
        s_rdy, p_rdy = sem("s_ready"), sem("p_ready")
        vt_rdy, vt_ev = sem("v_turned"), sem("v_ready")
        pv_rdy = sem("pv_ready")
        pv_use = sem("pv_used")
        ab_rdy = sem("abs_den_ready")
        h_rdy, hq_rdy = sem("h_ready"), sem("h_square_ready")
        hs_rdy, hr_rdy = sem("h_sum_ready"), sem("h_root_ready")
        hs_done = sem("head_done")
        nb_rdy = sem("neg_bias_ready")
        st_rdy, st_out = sem("gate_staged"), sem("gates_stored")
        cz = sem("glu_tail_zero")
        cv_done = sem("conv_done")
        ln_m, ln_c, ln_v, ln_n, ln_s = (sem(n) for n in ("ln_mean_ready", "ln_centred", "ln_var_ready", "ln_normed", "silu_done"))
        side_ld = [sem("side_loaded0"), sem("side_loaded1")]
        t_rdy = sem("t_ready")
        h_st = sem("h_stored")
        merged = sem("merged_ready")
        sc_rdy = sem("scores_ready")
        sc_use = sem("scores_used")
        sm_rdy, sm_exp = sem("softmax_in"), sem("softmax_exp")
        rt_done = sem("routing_done")
        tr_rdy, tr_ev, tr_ah = sem("tables_turned"), sem("tables_ready"), sem("a_hi_ready")
        hot_rdy, g_mm, g_ev = sem("one_hots_ready"), sem("g_ready"), sem("g_copied")
        g_st = [sem("g_stored0"), sem("g_stored1")]
        z_rdy = sem("z_staged")
        z_st = [sem("z_stored0"), sem("z_stored1")]
        o_ld = sem("h_reloaded")
        gg_ld = [sem("g_group_loaded0"), sem("g_group_loaded1")]
        zg_ld = [sem("z_group_loaded0"), sem("z_group_loaded1")]
        act_rdy = sem("act_ready")
        turns = [sem("turns_v"), sem("turns_p"), sem("turns_t")]
        out_rdy, out_st = sem("out_ready"), sem("out_stored")

        block = ctx.enter_context(nc.Block())
        r1f = R1[:, :, :].rearrange("p k t -> p (k t)")

        def r1tile(k):
            return r1f[:, k * T:k * T + T] if isinstance(k, int) else r1f[:, ds(k * T, T)]

        @block.sync
        def _(sp):
            def stream(src, nblocks, b0, first=0):
                with sp.Fori(0, (nblocks - first) // 2) as i:
                    for u in range(2):
                        sp.wait_ge(w_lo, b0 + first + u + 1 + 2 * i)
                        sp.dma_start(RAW[u][:, :], src[ds(2 * i + first + u, 1), :, :].rearrange("o p n -> (o p) n")
                                     ).then_inc(w_loaded[u], 16)

            for s in range(2):
                sp.sem_inc(g_st[s], 16)
            for s in range(4):
                sp.dma_start(R1[:, 4 * s:4 * s + 4, :], xT[:, 4 * s:4 * s + 4, :]).then_inc(x_ld[s], 16)
                if s == 0:
                    for dst, src in ((col, cols), (bias, bias_proj), (wg, w_gate), (bg, b_gate), (cw, conv_w), (sk, sub_keys)):
                        sp.dma_start(dst[:], src).then_inc(const_ld, 16)
            for u in range(2):
                sp.dma_start(RAW[u][:, :], w_proj[u]).then_inc(w_loaded[u], 16)
            stream(w_proj, NB_A1 + NB_A2, A1, first=2)
            stream(w_mo, NB_16, B1)
            stream(w_co, NB_16, B2)
            stream(w_o, NB_16, C1)
            stream(w_q, NB_16, Q1)
            def z_load(n):
                for u in range(2):
                    sp.wait_ge(w_lo, Z1 + u + 1 + n)
                    sp.dma_start(RAW[u][:, :], u_blocks[ds(n + u, 1), :, :].rearrange("o p n -> (o p) n")
                                 ).then_inc(w_loaded[u], 16)

            with sp.Fori(0, (Z_LOOK + 4) // 2) as i:
                z_load(2 * i)
            with sp.Fori(0, T // CH // 2) as cc:
                for half in range(2):
                    with sp.Fori(0, CH // TOK // 2) as m:
                        z_load(Z_LOOK + 4 + 16 * cc + 8 * half + 2 * m)
                    sp.wait_ge(g_ev, 32 * cc + 16 * half + 16)
                    sp.dma_start(g_dram[ds(2 * cc + half, 1), :, :].rearrange("o p n -> (o p) n"), GB[half][:, :]
                                 ).then_inc(g_st[half], 16)
            for s in range(2):
                sp.wait_ge(g_st[s], 8 * (T // CH) + 16)
            sp.wait_ge(h_st, 16)
            sp.dma_start(R2[:, :, :], h_dram.rearrange("p (k t) -> p k t", k=KT)).then_inc(o_ld, 16)
            with sp.Fori(0, (NB_E - Z_LOOK - 4 - Z_GATE) // 2) as i:
                z_load(Z_LOOK + 4 + Z_GATE + 2 * i)
            stream(v_blocks, NB_E, O1)
            for k in range(KT):
                sp.wait_ge(out_rdy, k + 1)
                sp.dma_start(out[:, k, :], R2[:, k, :]).then_inc(out_st, 16)
            sp.wait_ge(out_st, 16 * KT)
            sp.wait_ge(st_out, 16 * 2 * KT)
            sp.wait_ge(r_st, 64)
            for s in range(2):
                sp.wait_ge(z_st[s], 16 * NB_E // 2)

        @block.gpsimd
        def _(pool):
            pool.memset(ones[:], 1.0).then_inc(pool_const, 1)
            pool.memset(zer[:], 0.0).then_inc(pool_const, 1)
            pool.memset(ident[:], 0.0).then_inc(pool_const, 1)
            pool.wait_ge(pool_const, 3)
            pool.affine_select(out=ident[:], in_=ident[:], compare_op=ALU.not_equal, fill=1.0, base=0,
                               pattern=[[-1, P]], channel_multiplier=1).then_inc(pool_const, 1)
            pool.iota(iota[:], pattern=[[1, P]], base=0, channel_multiplier=0,
                      allow_small_or_imprecise_dtypes=True).then_inc(pool_const, 1)
            pool.wait_ge(g_row, 2)
            for r, dst in enumerate((gi[:, 0, :], gf[:, 0, :], gi[:, 1, :], gf[:, 1, :])):
                pool.dma_start(dst, gsb[8 * r:8 * r + 8, :]).then_inc(g_split, 16)
            pool.wait_ge(gv, 7)
            pool.wait_ge(ga_step, 5)
            for r, (t, d) in enumerate(((gM, 0), (gt, 0), (gM, 1), (gt, 1))):
                pool.dma_start(rows_dram[:, r, :], t[:, d, NM:L]).then_inc(r_st, 16)
            pool.wait_ge(r_st, 64)
            pool.wait_ge(u_rdy, KT)
            pool.wait_ge(g_split, 64)
            with pool.Fori(0, NH) as h:
                pool.wait_ge(pv_use, 4 * h)
                pool.dma_start(rows[:, :, :].rearrange("p a t -> p (a t)"),
                               rows_dram[ds(h, 1), :, :].rearrange("h a t -> h (a t)").to_broadcast((P, 4 * T))
                               ).then_inc(r_ld, 16)
                pool.wait_ge(e_exp, 3 * h + 3)
                pool.sem_inc(turns[1], 1)
                for j in range(TT):
                    f = PF[:, F_OFF[j]:F_OFF[j] + P]
                    pool.affine_select(out=f, in_=f, compare_op=ALU.is_ge, fill=0.0, base=0, pattern=[[1, P]],
                                       channel_multiplier=-1).then_inc(e_msk, 1)
                    q = PB[:, B_OFF[j] + P * j:B_OFF[j] + P * j + P]
                    pool.affine_select(out=q, in_=q, compare_op=ALU.is_ge, fill=0.0, base=0, pattern=[[-1, P]],
                                       channel_multiplier=1).then_inc(e_msk, 1)
            with pool.Fori(0, KT) as c:
                for g, (stage, dram) in enumerate(((st0, ga_dram), (st1, gb_dram))):
                    pool.wait_ge(evac_a, 6 * NH + 4 * c + 3 + g)
                    pool.sem_inc(turns[1], 1)
                    pool.dma_start(dram[ds(c, 1), :, :].rearrange("o p t -> (o p) t"), stage[:, :]).then_inc(st_out, 16)
            pool.wait_ge(st_out, 32 * KT)
            for ph, (src, e0) in enumerate(((ga_dram, 56), (gb_dram, 72), (None, 88))):
                with pool.Fori(0, KT // 2) as i:
                    for u in range(2):
                        pool.wait_ge(evac_v, e0 - 1 + u + 2 * i)
                        if src is not None:
                            s = src[ds(2 * i + u, 1), :, :].rearrange("o p t -> (o p) t")
                        else:
                            s = xT[:, ds(2 * i + u, 1), NM:L].rearrange("p o t -> p (o t)")
                        pool.dma_start(side[u][:, :], s).then_inc(side_ld[u], 16)
            pool.wait_ge(evac_v, 104)
            pool.dma_start(h_dram, r1f[:, 0:KT * T]).then_inc(h_st, 16)

            def z_store(n):
                for u in range(2):
                    pool.wait_ge(evac_a, n + (112 + u + 1))
                    pool.dma_start(z_dram[ds(n + u, 1), :, :].rearrange("o p t -> (o p) t"), zs[u][:, :]
                                   ).then_inc(z_st[u], 16)

            def group_load(g, par):
                pool.dma_start(ZG[par][:, :, :], z_dram[ds(g * GJ, GJ), :, :].rearrange("j p t -> p j t")
                               ).then_inc(zg_ld[par], 16)
                pool.dma_start(GG[par][:, :, :], g_dram[:, :, ds(g * (GJ * CH), GJ * CH)].rearrange("c p n -> p c n")
                               ).then_inc(gg_ld[par], 16)

            early = Z_LOOK + Z_GATE + 8
            with pool.Fori(0, early // 2) as i:
                z_store(2 * i)
            for s in range(2):
                pool.wait_ge(g_st[s], 8 * (T // CH) + 16)
                pool.wait_ge(z_st[s], 8 * early)
            group_load(0, 0)
            with pool.Fori(0, (NB_E - early) // 2) as i:
                z_store(2 * i + early)
            for s in range(2):
                pool.wait_ge(z_st[s], 8 * NB_E)
            group_load(1, 1)
            with pool.Fori(1, KEYS // GJ // 2) as gg:
                for par in range(2):
                    pool.wait_ge(x_lo, 16 * gg + (80 + 8 * par - 8))
                    pool.sem_inc(turns[1], 1)
                    group_load(2 * gg + par, par)

        @block.tensor
        def _(pe):
            def mm3(dst, whi, wlo, xhi, xlo, start, stop):
                pe.matmul(dst, whi, xhi, start=start, stop=False)
                pe.matmul(dst, whi, xlo, start=False, stop=False)
                return pe.matmul(dst, wlo, xhi, start=False, stop=stop)

            def blk(b, s, outs, waits, x0=None):
                pe.wait_ge(w_lo, b + 3)
                for k, (bank, c0, n) in enumerate(outs):
                    for ws, wv in waits[k]:
                        pe.wait_ge(ws, wv)
                    for kt in range(KT):
                        if x0 is not None and k == 0 and kt % 4 == 0:
                            pe.wait_ge(x_lo, x0 + kt + 4)
                        wcol = slice(kt * P, kt * P + P)
                        m = mm3(bank[:, 0:n], WH[s][:, wcol], WL[s][:, wcol], XH[:, kt, c0:c0 + n], XL[:, kt, c0:c0 + n],
                                kt == 0, kt == KT - 1)
                m.then_inc(w_used, 1)

            FULL = lambda a, b: [(a, 0, HALF), (b, HALF, HALF)]
            TOKS = lambda a: [(a, NM, T)]
            FLAT = lambda a: [(a, 0, T)]

            pe.sem_inc(w_used, 2)
            pe.wait_ge(pool_const, 5)
            for kt in range(KT):
                pe.wait_ge(sq_rdy, kt + 1)
                s = (sq0, sq1)[kt % 2]
                pe.matmul(A[0][:, 0:HALF], ones[:], s[:, 0:HALF], start=kt == 0, stop=kt == KT - 1)
                pe.matmul(A[1][:, 0:HALF], ones[:], s[:, HALF:L], start=kt == 0, stop=kt == KT - 1).then_inc(ss_use, 1)
            pe.wait_ge(const_ld, 96)
            for kt in range(KT):
                pe.wait_ge(u_rdy, kt + 1)
                pe.matmul(A[2][0:32, 0:HALF], wg[:, kt, :], R1[:, kt, 0:HALF], start=kt == 0, stop=kt == KT - 1)
                m = pe.matmul(A[3][0:32, 0:HALF], wg[:, kt, :], R1[:, kt, HALF:L], start=kt == 0, stop=kt == KT - 1)
            m.then_inc(g_rdy, 1)

            def c_columns():
                pe.wait_ge(gv, 7)
                for d in range(2):
                    for j in range(TT):
                        pe.transpose(A[4][:, (TT * d + j) * NH:(TT * d + j + 1) * NH],
                                     gi[:, d, NM + P * j:NM + P * j + P], ident[0:NH, 0:NH])
                pe.transpose(A[4][0:NM, 8 * NH:9 * NH], gi[:, 0, 0:NM], ident[0:NH, 0:NH]).then_inc(c_rdy, 1)

            def head(h, first):
                b = 6 * h
                blk(b, 0, TOKS(bk[0]), [[(evac_a, 6 * h)]], 0 if first else None)
                if first:
                    c_columns()
                blk(b + 1, 1, FULL(bk[1], bk[2]), [[], []])
                blk(b + 2, 0, FULL(bk[0], bk[1]), [[(evac_v, 3 * h + 1)], [(evac_v, 3 * h + 2)]])
                pe.wait_ge(evac_v, 3 * h + 3)
                pe.wait_ge(pv_use, 4 * h)
                pe.wait_ge(hr_rdy, h)
                for j in range(TT):
                    pe.matmul(A[j][:, :], kT[:, NM + P * j:NM + P * j + P], qT[:, :], start=True, stop=True).then_inc(s_rdy, 1)
                if first:
                    pe.wait_ge(c_ev, 2)
                pe.matmul(A[4][0:NM, :], kT[:, 0:NM], qT[:, :], start=True, stop=True).then_inc(s_rdy, 1)
                blk(b + 3, 1, FULL(bk[2], bk[0]), [[(evac_v, 3 * h + 3)], [(evac_a, 6 * h + 1)]])
                pe.wait_ge(evac_a, 6 * h + 4)
                pe.wait_ge(p_rdy, 9 * h + 9)
                for v in range(2):
                    for j in range(TT):
                        m = pe.transpose(A[v][:, P * j:P * j + P], vT[:, v, NM + P * j:NM + P * j + P], ident[:])
                    m.then_inc(vt_rdy, 1)
                for v in range(2):
                    m = pe.transpose(A[2][0:NM, P * v:P * v + P], vT[:, v, 0:NM], ident[:])
                m.then_inc(vt_rdy, 1)
                pe.wait_ge(vt_ev, 3 * h + 3)

                def fwd(bank, wm, w):
                    pe.matmul(bank[:, :], wm, PM[:, :], start=True, stop=False)
                    for j in range(TT):
                        m = pe.matmul(bank[:, P * j:T], w(j), PF[:, F_OFF[j]:F_OFF[j] + T - P * j],
                                      start=False, stop=j == TT - 1)
                    m.then_inc(pv_rdy, 1)

                def bwd(bank, w):
                    for j in reversed(range(TT)):
                        m = pe.matmul(bank[:, 0:P * j + P], w(j), PB[:, B_OFF[j]:B_OFF[j] + P * j + P],
                                      start=j == TT - 1, stop=j == 0)
                    m.then_inc(pv_rdy, 1)

                fwd(A[2], ones[0:NM, :], lambda j: ones[:])
                for v in range(2):
                    fwd(A[3 + v], VM[:, P * v:P * v + P], lambda j: V[:, j, P * v:P * v + P])
                for v in range(2):
                    bwd(A[v], lambda j: V[:, j, P * v:P * v + P])
                pe.wait_ge(ab_rdy, 2 * h + 1)
                bwd(A[2], lambda j: ones[:])
                blk(b + 4, 0, TOKS(bk[1]), [[(evac_a, 6 * h + 2)]])
                blk(b + 5, 1, TOKS(bk[2]), [[(evac_a, 6 * h + 3)]])
                pe.wait_ge(hq_rdy, 2 * h + 2)
                pe.wait_ge(ab_rdy, 2 * h + 2)
                pe.matmul(A[2][:, :], ones[:], hs_sq[:, 0, :], start=True, stop=False)
                pe.matmul(A[2][:, :], ones[:], hs_sq[:, 1, :], start=False, stop=True).then_inc(hs_rdy, 1)

            head(0, True)
            with pe.Fori(1, NH) as h:
                head(h, False)

            pe.wait_ge(evac_v, 3 * NH)
            with pe.Fori(0, KT) as c:
                b = A2 + 4 * c
                blk(b, 0, FULL(bk[0], bk[1]), [[(evac_v, 24 + 2 * c), (evac_a, 48 + 4 * c)], []])
                blk(b + 1, 1, FULL(bk[2], bk[0]), [[], [(evac_a, 48 + 4 * c + 1)]])
                blk(b + 2, 0, TOKS(bk[1]), [[(evac_a, 48 + 4 * c + 2)]])
                blk(b + 3, 1, TOKS(bk[2]), [[(evac_v, 24 + 2 * c + 1)]])

            def pair(b0, e0, n, x0=None):
                for u in range(2):
                    blk(b0 + u + n, u, FLAT(bk[u]), [[(evac_v, e0 - 1 + u + n)]], x0 if u == 0 else None)

            pe.wait_ge(evac_a, 112)
            pair(B1, 56, 0, 16)
            pe.wait_ge(cv_done, KT)
            for k in range(KT):
                m = pe.matmul(A[0][:, :], ones[:], r1tile(k),
                              start=k == 0, stop=k == KT - 1)
            m.then_inc(ln_m, 1)
            with pe.Fori(1, 4) as i:
                pair(B1, 56, 2 * i)
            for k in range(KT):
                pe.wait_ge(sq_rdy, KT + k + 1)
                pe.matmul(A[1][:, :], ones[:], SQ[k % 4][:, :], start=k == 0, stop=k == KT - 1).then_inc(ss_use, 1)
            with pe.Fori(4, 8) as i:
                pair(B1, 56, 2 * i)
            pair(B2, 72, 0, 32)
            with pe.Fori(1, 8) as i:
                pair(B2, 72, 2 * i)

            def hsum(n, u, last=False):
                pe.wait_ge(sq_rdy, n + (2 * KT + 1))
                pe.matmul(A[0][:, :], ones[:], SQ[u][:, :], start=False, stop=last, skip_group_check=True).then_inc(ss_use, 1)

            for q in range(TT):
                pe.matmul(A[0][:, P * q:P * q + P], zer[:], ident[:], start=q == 0, stop=False, skip_group_check=True)
            pair(C1, 88, 0, 48)
            hsum(0, 0)
            with pe.Fori(1, 8) as i:
                blk(C1 + 2 * i, 0, FLAT(bk[0]), [[(evac_v, 87 + 2 * i)]])
                hsum(2 * i - 1, 1)
                blk(C1 + 1 + 2 * i, 1, FLAT(bk[1]), [[(evac_v, 88 + 2 * i)]])
                hsum(2 * i, 0)
            hsum(15, 1, True)

            def scores(n, u):
                pe.wait_ge(evac_v, n + 105)
                if not (isinstance(n, int) and n < 2):
                    pe.wait_ge(sc_use, n - 1)
                for t in range(TT):
                    m = pe.matmul(A[1 + u][:, P * t:P * t + P], qry[u][:, P * t:P * t + P], sk[:, u, :],
                                  start=t == 0, stop=t == TT - 1, skip_group_check=True)
                m.then_inc(sc_rdy, 1)

            pair(Q1, 104, 0, 64)
            scores(0, 0)
            with pe.Fori(1, 8) as i:
                blk(Q1 + 2 * i, 0, FLAT(bk[0]), [[(evac_v, 103 + 2 * i)]])
                scores(2 * i - 1, 1)
                blk(Q1 + 1 + 2 * i, 1, FLAT(bk[1]), [[(evac_v, 104 + 2 * i)]])
                scores(2 * i, 0)
            scores(15, 1)

            def zpair(n):
                for u in range(2):
                    blk(Z1 + u + n, u, FLAT(bk[u]), [[(evac_a, 111 + u + n)]])

            pe.wait_ge(evac_v, 120)
            with pe.Fori(0, Z_LOOK // 2) as i:
                zpair(2 * i)
            pe.wait_ge(rt_done, 1)
            for k, src in enumerate((EI, EJ, GA)):
                for t in range(TT):
                    m = pe.transpose(A[k][:, P * t:P * t + P], src[:, t, :], ident[:])
                m.then_inc(tr_rdy, 1)
            pe.wait_ge(tr_ev, 3)
            with pe.Fori(0, Z_GATE // 2) as i:
                for u in range(2):
                    blk(Z1 + Z_LOOK + u + 2 * i, u, FLAT(bk[u]), [[(evac_a, 111 + Z_LOOK + u + 2 * i)]])
                    for g in range(2):
                        pe.wait_ge(hot_rdy, 4 * i + 2 * u + g + 1)
                        pe.wait_ge(g_ev, 4 * i)
                        hi_, jh, jl = hot[3 * g:3 * g + 3]
                        bank = A[2 * u + g]
                        for q in range(4):
                            o = bank[:, P * q:P * q + P]
                            pe.matmul(o, hi_[:, q, :], jh[:, q, :], start=q == 0, stop=False, skip_group_check=True)
                            m = pe.matmul(o, hi_[:, q, :], jl[:, q, :], start=False, stop=q == 3, skip_group_check=True)
                        m.then_inc(g_mm, 1)
            with pe.Fori(0, (NB_E - Z_LOOK - Z_GATE) // 2) as i:
                zpair(Z_LOOK + Z_GATE + 2 * i)

            pe.wait_ge(evac_a, 112 + NB_E)
            pe.wait_ge(g_ev, 2 * Z_GATE)
            obank = [[bk[0], bk[1]], [bk[2], A[0]]]
            with pe.Fori(0, KEYS // GJ // 2) as gg:
                for par in range(2):
                    pe.wait_ge(x_lo, 80 + 8 * par + 8 + 16 * gg)
                    pe.sem_inc(turns[2], 1)
                    with pe.Fori(0, 4) as m_:
                        for u in range(2):
                            n = 16 * gg + 8 * par + 2 * m_ + u
                            pe.wait_ge(w_lo, n + (O1 + 3))
                            pe.wait_ge(evac_v, 2 * n + (120 - 2))
                            for k in range(2):
                                for jj in range(GJ):
                                    wcol = slice(jj * 256 + k * P, jj * 256 + k * P + P)
                                    m = mm3(obank[u][k][:, :], WH[u][:, wcol], WL[u][:, wcol],
                                            XH[:, GJ * par + jj, 0:T], XL[:, GJ * par + jj, 0:T], jj == 0, jj == GJ - 1)
                            m.then_inc(w_used, 1)
            for k in range(KT):
                pe.wait_ge(sq_rdy, 3 * KT + k + 1)
                pe.matmul(A[1][:, :], ones[:], SQ[k % 4][:, :], start=k == 0, stop=k == KT - 1).then_inc(ss_use, 1)

        @block.scalar
        def _(act):
            def hi(n_slot, b, s):
                act.wait_ge(w_loaded[s], n_slot)
                act.wait_ge(w_used, b + 1)
                act.activation(WH[s][:, :], RAW[s][:, :], ACT.Copy).then_inc(w_hi, 1)

            def hi2(b0, n, u):
                hi(8 * n + (8 * (b0 + 2) + 16), n + (b0 + 2 + u), u)

            for kt in range(KT):
                act.wait_ge(x_ld[kt // 4], 16)
                if kt >= 2:
                    act.wait_ge(ss_use, kt - 1)
                act.activation((sq0, sq1)[kt % 2][:, :], R1[:, kt, :], ACT.Square).then_inc(sq_rdy, 1)
            act.wait_ge(const_ld, 96)
            act.wait_ge(ss_use, KT)
            act.activation(rb1[:, 0:HALF], A[0][:, 0:HALF], ACT.Sqrt, bias=col[:, EPSC, 0:1], scale=1.0 / D).then_inc(rt_rdy, 1)
            act.activation(rb1[:, HALF:L], A[1][:, 0:HALF], ACT.Sqrt, bias=col[:, EPSC, 0:1], scale=1.0 / D).then_inc(rt_rdy, 1)
            hi(16, 0, 0)
            for kt in range(KT):
                act.wait_ge(u_rdy, kt + 1)
                act.activation(XH[:, kt, :], R1[:, kt, :], ACT.Copy).then_inc(x_hi, 1)
                if kt == 8:
                    hi(16, 1, 1)
            act.wait_ge(g_split, 64)
            act.activation(gt[:, :, :], gf[:, :, :], ACT.Abs).then_inc(ga_step, 1)
            act.wait_ge(ga_step, 1)
            act.activation(gt[:, :, :], gt[:, :, :], ACT.Exp, scale=-1.0).then_inc(ga_step, 1)
            act.wait_ge(ga_step, 2)
            act.activation(gt[:, :, :], gt[:, :, :], ACT.Ln, bias=1.0).then_inc(ga_step, 1)
            act.wait_ge(gv, 7)
            for d in range(2):
                act.activation(gt[:, d, NM:L], gt[:, d, NM:L], ACT.Exp, scale=-1.0).then_inc(ga_step, 1)

            with act.Fori(0, NH) as h:
                b = 6 * h

                def nxt(u):
                    hi2(A1 + u // 2 * 2, 6 * h, u % 2)

                act.wait_ge(w_used, b + 3)
                nxt(0)
                act.wait_ge(w_used, b + 4)
                nxt(1)
                act.wait_ge(e_rdy, 9 * h + 9)
                act.activation(PF[:, :], PF[:, :], ACT.Exp).then_inc(e_exp, 1)
                act.activation(PB[:, :], PB[:, :], ACT.Exp).then_inc(e_exp, 1)
                act.activation(PM[:, :], PM[:, :], ACT.Exp).then_inc(e_exp, 1)
                for v, banks in enumerate(((bk[0], bk[1]), (bk[2], bk[0]))):
                    act.wait_ge(w_used, b + 5 + v)
                    act.wait_ge(vt_rdy, 3 * h)
                    for k in range(2):
                        act.activation(vT[:, v, HALF * k:HALF * k + HALF], banks[k][:, 0:HALF], ACT.Identity,
                                       bias=bias[:, ds(b + 2 + v, 1)]).then_inc(evac_a, 1)
                    nxt(2 + v)
                act.wait_ge(pv_rdy, 6 * h)
                for v in range(2):
                    act.wait_ge(vt_rdy, 3 * h + v + 1)
                    act.activation(V[:, :, P * v:P * v + P], A[v][:, :].rearrange("p (j q) -> p j q", j=TT), ACT.Copy
                                   ).then_inc(vt_ev, 1)
                act.wait_ge(vt_rdy, 3 * h + 3)
                act.activation(VM[:, :], A[2][0:NM, 0:2 * P], ACT.Copy).then_inc(vt_ev, 1)
                act.wait_ge(pv_rdy, 6 * h + 1)
                act.wait_ge(pv_use, 4 * h)
                act.activation(dF[:, :], A[2][:, :], ACT.Abs).then_inc(ab_rdy, 1)
                act.wait_ge(pv_rdy, 6 * h + 6)
                act.activation(dB[:, :], A[2][:, :], ACT.Abs).then_inc(ab_rdy, 1)
                act.wait_ge(nb_rdy, 1)
                act.wait_ge(hs_done, 2 * h)
                act.wait_ge(w_used, b + 7)
                act.activation(og[:, 0, :], bk[1][:, :], ACT.Exp, scale=-1.0, bias=nbias[:, ds(b + 4, 1)]).then_inc(evac_a, 1)
                nxt(4)
                for v in range(2):
                    act.wait_ge(h_rdy, 2 * h + v + 1)
                    act.activation(hs_sq[:, v, :], hh[:, v, :], ACT.Square).then_inc(hq_rdy, 1)
                act.wait_ge(w_used, b + 8)
                act.activation(og[:, 1, :], bk[2][:, :], ACT.Exp, scale=-1.0, bias=nbias[:, ds(b + 5, 1)]).then_inc(evac_a, 1)
                nxt(5)
                act.wait_ge(hs_rdy, h + 1)
                act.activation(rs_h[:, :], A[2][:, :], ACT.Sqrt, bias=col[:, EPSC, 0:1], scale=1.0 / 256).then_inc(hr_rdy, 1)

            act.wait_ge(hs_done, 2 * NH)
            act.wait_ge(pv_use, 4 * NH)
            with act.Fori(0, KT) as c:
                b = A2 + 4 * c
                act.wait_ge(evac_v, 24 + 2 * c)
                act.wait_ge(w_used, b + 3)
                for k in range(2):
                    act.activation(sg[:, HALF * k:HALF * k + HALF], bk[k][:, 0:HALF], ACT.Sigmoid,
                                   bias=bias[:, ds(b, 1)]).then_inc(evac_a, 1)
                hi2(A2, 4 * c, 0)
                act.wait_ge(w_used, b + 4)
                hi2(A2, 4 * c, 1)
                act.wait_ge(st_out, 32 * c)
                for g, (stage, bank) in enumerate(((st0, bk[1]), (st1, bk[2]))):
                    act.wait_ge(w_used, b + 5 + g)
                    act.activation(stage[:, :], bank[:, :], ACT.Sigmoid, bias=bias[:, ds(b + 2 + g, 1)]).then_inc(evac_a, 1)
                    hi2(A2 + 2, 4 * c, g)

            def split_x(src, phase, x0):
                act.wait_ge(w_used, phase + 2)
                for k in range(KT):
                    act.activation(XH[:, k, 0:T], src(k), ACT.Copy).then_inc(x_hi, 1)

            r2t = lambda k: R2[:, k, :]

            def follow(b0, n):
                for u in range(2):
                    act.wait_ge(w_used, b0 + u + 3 + n)
                    hi2(b0, n, u)

            act.wait_ge(hs_done, 2 * NH)
            split_x(r2t, B1, 16)
            with act.Fori(0, 4) as i:
                follow(B1, 2 * i)
            for k in range(KT):
                act.wait_ge(ln_c, k + 1)
                if k >= 4:
                    act.wait_ge(ss_use, KT + k - 3)
                act.activation(SQ[k % 4][:, :], r1tile(k), ACT.Square).then_inc(sq_rdy, 1)
            act.wait_ge(ss_use, 2 * KT)
            act.activation(rsB[:, :], A[1][:, :], ACT.Sqrt, bias=col[:, EPSC, 0:1], scale=1.0 / D).then_inc(rt_rdy, 1)
            follow(B1, 8)
            for k in range(KT):
                act.wait_ge(ln_n, k + 1)
                act.activation(r1tile(k), r1tile(k), ACT.Silu, scale=col[:, LNW, k:k + 1], bias=col[:, LNB, k:k + 1]).then_inc(ln_s, 1)
                if k % 8 == 7:
                    follow(B1, 10 + k // 8 * 2)
            follow(B1, 14)
            act.wait_ge(ln_s, KT)
            split_x(r1tile, B2, 32)
            with act.Fori(0, 8) as i:
                follow(B2, 2 * i)
            act.wait_ge(merged, KT)
            split_x(r2t, C1, 48)
            with act.Fori(0, 8) as i:
                for u in range(2):
                    act.wait_ge(evac_v, 88 + u + 1 + 2 * i)
                    act.wait_ge(ss_use, 31 + u + 2 * i)
                    act.activation(SQ[u][:, :], r1tile(2 * i + u), ACT.Square).then_inc(sq_rdy, 1)
                    hi2(C1, 2 * i, u)
            act.wait_ge(ss_use, 3 * KT)
            act.activation(rsB[:, :], A[0][:, :], ACT.Sqrt, bias=col[:, EPSC, 0:1], scale=1.0 / D).then_inc(rt_rdy, 1)
            act.wait_ge(w_used, Q1 + 2)
            for k in range(KT):
                act.wait_ge(t_rdy, k + 1)
                act.activation(XH[:, k, 0:T], SQ[k % 4][:, :], ACT.Copy).then_inc(x_hi, 1)
            with act.Fori(0, 8) as i:
                follow(Q1, 2 * i)
            act.wait_ge(sm_rdy, 1)
            act.activation(GA[:, :, :], GA[:, :, :], ACT.Exp).then_inc(sm_exp, 1)

            def zevac(n, u, st):
                act.wait_ge(w_used, Z1 + u + 3 + n)
                act.wait_ge(z_st[u], st)
                act.activation(zs[u][:, :], bk[u][:, :], ACT.Gelu_apprx_tanh).then_inc(evac_a, 1)
                hi2(Z1, n, u)

            with act.Fori(0, Z_LOOK // 2) as i:
                for u in range(2):
                    zevac(2 * i, u, 16 * i)
            act.wait_ge(tr_rdy, 3)
            act.activation(AH[:, :], A[2][:, :], ACT.Copy).then_inc(tr_ah, 1)
            act.wait_ge(tr_ah, 1)
            act.wait_ge(h_st, 16)
            with act.Fori(0, T // CH // 2) as cc:
                for half in range(2):
                    with act.Fori(0, CH // TOK // 2) as m_:
                        for u in range(2):
                            n = 16 * cc + 8 * half + 2 * m_
                            zevac(n + Z_LOOK, u, 8 * (16 * cc + 8 * half + 2 * m_) + 8 * Z_LOOK)
                            for g in range(2):
                                act.wait_ge(g_mm, 32 * cc + 16 * half + 4 * m_ + (2 * u + g + 1))
                                act.wait_ge(g_st[half], 16 * cc + 16)
                                dst = GB[half][:, :].rearrange("p (j t) -> p t j", t=CH)
                                act.activation(dst[:, ds(16 * m_ + (8 * u + 4 * g), 4), :],
                                               A[2 * u + g][:, :].rearrange("p (t j) -> p t j", t=4), ACT.Copy
                                               ).then_inc(g_ev, 1)
            with act.Fori(0, (NB_E - Z_LOOK - Z_GATE) // 2) as i:
                for u in range(2):
                    zevac(2 * i + (Z_LOOK + Z_GATE), u, 16 * i + 8 * (Z_LOOK + Z_GATE))
            def act_hi(par, jj, cnt, free):
                act.wait_ge(act_rdy, cnt)
                act.wait_ge(w_used, free)
                act.activation(XH[:, GJ * par + jj, 0:T], ZG[par][:, jj, :], ACT.Copy).then_inc(x_hi, 1)

            for jj in range(GJ):
                act_hi(0, jj, jj + 1, O1 + 2)

            def ogroup(gg, par, more, tail):
                for r in range(8):
                    b = O1 + 8 * par + r
                    u = r % 2
                    if more:
                        act_hi(1 - par, r, 16 * gg + (8 * par + 8 + r + 1), 16 * gg + (O1 + 8 * par + 2))
                    act.wait_ge(w_used, 16 * gg + (b + 3))
                    if not (tail and r >= 6):
                        hi2(O1 + 8 * par + r - u, 16 * gg, u)

            with act.Fori(0, 7) as gg:
                ogroup(gg, 0, True, False)
                ogroup(gg, 1, True, False)
            ogroup(7, 0, True, False)
            ogroup(7, 1, False, True)
            for k in range(KT):
                act.wait_ge(evac_v, 120 + 2 * NB_E - KT + k + 1)
                if k >= 4:
                    act.wait_ge(ss_use, 3 * KT + k - 3)
                act.activation(SQ[k % 4][:, :], R2[:, k, :], ACT.Square).then_inc(sq_rdy, 1)
            act.wait_ge(ss_use, 4 * KT)
            act.activation(rsB[:, :], A[1][:, :], ACT.Sqrt, bias=col[:, EPSC, 0:1], scale=1.0 / D).then_inc(rt_rdy, 1)

        @block.vector
        def _(dve):
            chain = {"base": 0, "i": None, "per": 0, "k": 0}

            def here():
                v = chain["base"] + chain["k"]
                return v if chain["i"] is None else chain["i"] * chain["per"] + v

            def step(ins):
                ins.then_inc(v_step, 1)
                chain["k"] += 1
                return here()

            def link(ins):
                dve.wait_ge(v_step, step(ins))

            def loop(i, per):
                chain.update(base=here(), i=i, per=per, k=0)

            def done(n):
                assert chain["k"] == chain["per"], chain
                chain.update(base=chain["base"] + n * chain["per"], i=None, k=0)

            def stand():
                dve.sem_inc(turns[0], 1)

            def lo(b, s):
                dve.wait_ge(w_hi, b + 1)
                dve.tensor_tensor(WL[s][:, :], RAW[s][:, :], WH[s][:, :].bitcast(F32), ALU.subtract).then_inc(w_lo, 1)

            dve.sem_inc(w_lo, 2)
            dve.wait_ge(rt_rdy, 2)
            link(dve.reciprocal(rb1[:, :], rb1[:, :]))
            dve.wait_ge(const_ld, 96)
            for kt in range(KT):
                dve.scalar_tensor_tensor(R1[:, kt, :], R1[:, kt, :], col[:, N1W, kt:kt + 1], rb1[:, :], ALU.mult, ALU.mult
                                         ).then_inc(u_rdy, 1)
                if kt == 1:
                    lo(0, 0)
                if kt >= 1:
                    dve.wait_ge(x_hi, kt)
                    dve.tensor_tensor(XL[:, kt - 1, :], R1[:, kt - 1, :], XH[:, kt - 1, :].bitcast(F32), ALU.subtract).then_inc(x_lo, 1)
            dve.wait_ge(x_hi, KT)
            dve.tensor_tensor(XL[:, KT - 1, :], R1[:, KT - 1, :], XH[:, KT - 1, :].bitcast(F32), ALU.subtract).then_inc(x_lo, 1)
            lo(1, 1)
            dve.tensor_scalar(nbias[:, :], bias[:, 0:NB_A1], -1.0, None, ALU.mult).then_inc(nb_rdy, 1)
            dve.wait_ge(g_rdy, 1)
            dve.tensor_scalar(gsb[:, 0:HALF], A[2][0:32, 0:HALF], bg[:, 0:1], None, ALU.add).then_inc(g_row, 1)
            dve.tensor_scalar(gsb[:, HALF:L], A[3][0:32, 0:HALF], bg[:, 0:1], None, ALU.add).then_inc(g_row, 1)
            link(dve.memset(gz[:, :], 0.0))
            dve.wait_ge(g_split, 64)
            dve.wait_ge(ga_step, 3)
            dve.scalar_tensor_tensor(gf[:, :, :], gf[:, :, :], 0.0, gt[:, :, :], ALU.min, ALU.subtract).then_inc(gv, 1)
            dve.wait_ge(gv, 1)
            back = slice(L - 1, NM - 1, -1)
            dve.tensor_tensor_scan(gF[:, 0, :], gf[:, 0, :], gz[:, :], 0.0, ALU.add, ALU.add).then_inc(gv, 1)
            dve.tensor_tensor_scan(gF[:, 1, back], gf[:, 1, back], gz[:, back], 0.0, ALU.add, ALU.add).then_inc(gv, 1)
            dve.wait_ge(gv, 3)
            dve.tensor_tensor(gi[:, 0, :], gi[:, 0, :], gF[:, 0, :], ALU.subtract).then_inc(gv, 1)
            dve.tensor_tensor(gi[:, 1, NM:L], gi[:, 1, NM:L], gF[:, 1, NM:L], ALU.subtract).then_inc(gv, 1)
            dve.wait_ge(gv, 5)
            link(dve.tensor_tensor_scan(gM[:, 0, :], gi[:, 0, :], gi[:, 0, :], 0.0, ALU.max, ALU.max))
            link(dve.tensor_tensor_scan(gM[:, 1, back], gi[:, 1, back], gi[:, 1, back], 0.0, ALU.max, ALU.max))
            link(dve.tensor_tensor(gt[:, 0, NM:L], gF[:, 0, NM:L], gM[:, 0, NM:L], ALU.add))
            link(dve.tensor_tensor(gt[:, 1, NM:L], gF[:, 1, NM:L], gM[:, 1, NM:L], ALU.add))
            for d in range(2):
                dve.tensor_scalar(gM[:, d, NM:L], gM[:, d, NM:L], -1.0, None, ALU.mult).then_inc(gv, 1)
            dve.wait_ge(c_rdy, 1)
            dve.tensor_copy(cT[:, :, :, :].rearrange("p d j h -> p (d j h)"), A[4][:, 0:8 * NH]).then_inc(c_ev, 1)
            dve.tensor_copy(cM[:, :], A[4][0:NM, 8 * NH:9 * NH]).then_inc(c_ev, 1)
            dve.wait_ge(c_ev, 2)

            with dve.Fori(0, NH) as h:
                loop(h, 11)
                b = 6 * h
                dve.wait_ge(w_used, b + 3)
                dve.wait_ge(s_rdy, 5 * h)
                dve.tensor_scalar(qT[:, :], bk[0][:, :], bias[:, ds(b, 1)], QSCALE, ALU.add, ALU.mult).then_inc(evac_v, 1)
                lo(b + 2, 0)
                dve.wait_ge(w_used, b + 4)
                for k in range(2):
                    dve.tensor_scalar(kT[:, HALF * k:HALF * k + HALF], bk[1 + k][:, 0:HALF], bias[:, ds(b + 1, 1)], None,
                                      ALU.add).then_inc(evac_v, 1)
                lo(b + 3, 1)
                dve.wait_ge(r_ld, 16 * h + 16)
                dve.wait_ge(pv_rdy, 6 * h)
                for j in range(TT):
                    w = T - P * j
                    dve.tensor_scalar(PF[:, F_OFF[j]:F_OFF[j] + w], rows[:, 0, P * j:T], cT[:, 0, j, ds(h, 1)], 0.0,
                                      ALU.add, ALU.min).then_inc(e_rdy, 1)
                    w = P * j + P
                    dve.tensor_scalar(PB[:, B_OFF[j]:B_OFF[j] + w], rows[:, 2, 0:w], cT[:, 1, j, ds(h, 1)], 0.0,
                                      ALU.add, ALU.min).then_inc(e_rdy, 1)
                dve.tensor_scalar(PM[:, :], rows[0:NM, 0, :], cM[:, ds(h, 1)], 0.0, ALU.add, ALU.min).then_inc(e_rdy, 1)
                dve.wait_ge(w_used, b + 5)
                lo(b + 4, 0)
                dve.wait_ge(e_exp, 3 * h + 3)
                dve.wait_ge(e_msk, 8 * h + 8)
                for j in range(TT):
                    dve.wait_ge(s_rdy, 5 * h + j + 1)
                    f = PF[:, F_OFF[j]:F_OFF[j] + T - P * j]
                    dve.tensor_tensor(f, f, A[j][:, P * j:T], ALU.mult).then_inc(p_rdy, 1)
                    g = PB[:, B_OFF[j]:B_OFF[j] + P * j + P]
                    dve.tensor_tensor(g, g, A[j][:, 0:P * j + P], ALU.mult).then_inc(p_rdy, 1)
                dve.wait_ge(s_rdy, 5 * h + 5)
                dve.tensor_tensor(PM[:, :], PM[:, :], A[4][0:NM, :], ALU.mult).then_inc(p_rdy, 1)
                dve.wait_ge(w_used, b + 6)
                lo(b + 5, 1)
                dve.wait_ge(ab_rdy, 2 * h + 1)
                link(dve.tensor_tensor(dF[:, :], dF[:, :], rows[:, 1, :], ALU.max))
                link(dve.reciprocal(dF[:, :], dF[:, :]))
                dve.wait_ge(hq_rdy, 2 * h)
                for v in range(2):
                    dve.wait_ge(pv_rdy, 6 * h + 2 + v)
                    dve.tensor_tensor(hh[:, v, :], A[3 + v][:, :], dF[:, :], ALU.mult).then_inc(pv_use, 1)
                dve.wait_ge(ab_rdy, 2 * h + 2)
                link(dve.tensor_tensor(dB[:, :], dB[:, :], rows[:, 3, :], ALU.max))
                link(dve.reciprocal(dB[:, :], dB[:, :]))
                for v in range(2):
                    dve.wait_ge(pv_rdy, 6 * h + 4 + v)
                    dve.tensor_tensor(hb[:, v, :], A[v][:, :], dB[:, :], ALU.mult).then_inc(pv_use, 1)
                dve.wait_ge(pv_use, 4 * h + 4)
                for v in range(2):
                    dve.tensor_tensor(hh[:, v, :], hh[:, v, :], hb[:, v, :], ALU.add).then_inc(h_rdy, 1)
                dve.wait_ge(w_used, b + 7)
                lo(b + 6, 0)
                dve.wait_ge(evac_a, 6 * h + 5)
                link(dve.tensor_scalar(og[:, 0, :], og[:, 0, :], 1.0, None, ALU.add))
                link(dve.reciprocal(og[:, 0, :], og[:, 0, :]))
                dve.wait_ge(w_used, b + 8)
                lo(b + 7, 1)
                dve.wait_ge(evac_a, 6 * h + 6)
                link(dve.tensor_scalar(og[:, 1, :], og[:, 1, :], 1.0, None, ALU.add))
                link(dve.reciprocal(og[:, 1, :], og[:, 1, :]))
                dve.wait_ge(hr_rdy, h + 1)
                dve.wait_ge(h_rdy, 2 * h + 2)
                link(dve.reciprocal(rs_h[:, :], rs_h[:, :]))
                for v in range(2):
                    link(dve.scalar_tensor_tensor(hh[:, v, :], hh[:, v, :], col[:, MNW, ds(2 * h + v, 1)], rs_h[:, :],
                                                  ALU.mult, ALU.mult))
                for v in range(2):
                    dve.tensor_tensor(R2[:, ds(2 * h + v, 1), :].rearrange("p o t -> p (o t)"), hh[:, v, :], og[:, v, :],
                                      ALU.mult).then_inc(hs_done, 1)
                done(NH)

            dve.wait_ge(hs_done, 2 * NH)
            link(dve.memset(cb[:, L:], 0.0))
            with dve.Fori(0, KT) as c:
                loop(c, CW - 1)
                b = A2 + 4 * c
                lo(b + 2, 0)
                dve.wait_ge(w_used, b + 4)
                dve.wait_ge(evac_a, 4 * c + (48 + 2))
                dve.wait_ge(cv_done, c)
                for k, bank in enumerate((bk[2], bk[0])):
                    dve.scalar_tensor_tensor(cb[:, HALF * k:HALF * k + HALF], bank[:, 0:HALF], bias[:, ds(b + 1, 1)],
                                             sg[:, HALF * k:HALF * k + HALF], ALU.add, ALU.mult).then_inc(evac_v, 1)
                lo(b + 3, 1)
                dve.wait_ge(evac_v, 2 * c + 26)
                acc = r1tile(c)
                link(dve.tensor_scalar(acc, cb[:, 1:1 + T], cw[:, ds(c * CW, 1)], col[:, CB, ds(c, 1)], ALU.mult, ALU.add))
                for k in range(1, CW):
                    tap = dve.scalar_tensor_tensor(acc, cb[:, 1 + k:1 + k + T], cw[:, ds(c * CW + k, 1)], acc,
                                                   ALU.mult, ALU.add)
                    if k < CW - 1:
                        link(tap)
                    else:
                        tap.then_inc(cv_done, 1)
                    if k in (10, 20):
                        lo(b + 4 + k // 10 - 1, k // 10 - 1)
                done(KT)

            def split_x(src, x0):
                for k in range(KT):
                    dve.wait_ge(x_hi, x0 + k + 1)
                    dve.tensor_tensor(XL[:, k, 0:T], src(k), XH[:, k, 0:T].bitcast(F32), ALU.subtract).then_inc(x_lo, 1)

            def r2tile(k):
                return R2[:, k, :] if isinstance(k, int) else R2[:, ds(k, 1), :].rearrange("p o t -> p (o t)")

            def b1(n, i, u):
                dve.wait_ge(w_used, n + (B1 + 3))
                dve.wait_ge(side_ld[u], 16 * i + 16)
                dve.tensor_tensor(r2tile(n), bk[u][:, :], side[u][:, :], ALU.mult).then_inc(evac_v, 1)
                lo(n + (B1 + 2), u)

            split_x(r2tile, 16)
            b1(0, 0, 0)
            b1(1, 0, 1)
            dve.wait_ge(ln_m, 1)
            dve.wait_ge(cv_done, KT)
            for k in range(KT):
                dve.scalar_tensor_tensor(r1tile(k), A[0][:, :], -1.0 / D, r1tile(k), ALU.mult, ALU.add).then_inc(ln_c, 1)
            with dve.Fori(1, 5) as i:
                for u in range(2):
                    b1(2 * i + u, i, u)
            dve.wait_ge(rt_rdy, 3)
            link(dve.reciprocal(rsB[:, :], rsB[:, :]))
            dve.wait_ge(ln_c, KT)
            for k in range(KT):
                dve.tensor_tensor(r1tile(k), r1tile(k), rsB[:, :], ALU.mult).then_inc(ln_n, 1)
                if k == 7:
                    for u in range(2):
                        b1(10 + u, 5, u)
            with dve.Fori(6, 8) as i:
                for u in range(2):
                    b1(2 * i + u, i, u)
            split_x(r1tile, 32)
            with dve.Fori(0, 8) as i:
                for u in range(2):
                    n = 2 * i + u
                    dve.wait_ge(w_used, n + (B2 + 3))
                    dve.wait_ge(side_ld[u], 16 * i + (16 + 128))
                    dve.wait_ge(merged, n)
                    dve.scalar_tensor_tensor(tmpB[:, :], bk[u][:, :], col[:, BCO, ds(n, 1)], side[u][:, :],
                                             ALU.add, ALU.mult).then_inc(evac_v, 1)
                    dve.wait_ge(evac_v, n + 73)
                    dve.tensor_tensor(r2tile(n), r2tile(n), tmpB[:, :], ALU.add).then_inc(merged, 1)
                    lo(n + (B2 + 2), u)
            split_x(r2tile, 48)
            with dve.Fori(0, 8) as i:
                for u in range(2):
                    n = 2 * i + u
                    dve.wait_ge(w_used, n + (C1 + 3))
                    dve.wait_ge(side_ld[u], 16 * i + (16 + 256))
                    dve.tensor_tensor(r1tile(n), bk[u][:, :], side[u][:, :], ALU.add).then_inc(evac_v, 1)
                    lo(n + (C1 + 2), u)
            dve.wait_ge(rt_rdy, 4)
            link(dve.reciprocal(rsB[:, :], rsB[:, :]))
            for k in range(KT):
                if k >= 4:
                    dve.wait_ge(x_lo, 64 + k - 3)
                dve.scalar_tensor_tensor(SQ[k % 4][:, :], r1tile(k), col[:, N2W, k:k + 1], rsB[:, :], ALU.mult, ALU.mult
                                         ).then_inc(t_rdy, 1)
                if k >= 1:
                    dve.wait_ge(x_hi, 64 + k)
                    dve.tensor_tensor(XL[:, k - 1, 0:T], SQ[(k - 1) % 4][:, :], XH[:, k - 1, 0:T].bitcast(F32), ALU.subtract
                                      ).then_inc(x_lo, 1)
            dve.wait_ge(x_hi, 80)
            dve.tensor_tensor(XL[:, KT - 1, 0:T], SQ[(KT - 1) % 4][:, :], XH[:, KT - 1, 0:T].bitcast(F32), ALU.subtract
                              ).then_inc(x_lo, 1)

            def query(n, u, first):
                dve.wait_ge(w_used, n + (Q1 + 3))
                if not first:
                    dve.wait_ge(sc_rdy, n - 1)
                dve.tensor_copy(qry[u][:, :], bk[u][:, :]).then_inc(evac_v, 1)
                lo(n + (Q1 + 2), u)

            def top16(src, rest, vals, idx, n, last=None):
                stand()
                a = [step(dve.max(vals[:, t, 0:8], src(t))) for t in range(TT)]
                for t in range(TT):
                    dve.wait_ge(v_step, a[t])
                    stand()
                    step(dve.max_index(idx[:, t, 0:8], vals[:, t, 0:8], src(t)))
                a = [step(dve.match_replace(rest[:, t, :], vals[:, t, 0:8], src(t), NEG)) for t in range(TT)]
                if last is not None:
                    dve.wait_ge(v_step, a[-1])
                    dve.sem_inc(last, 1)
                c = []
                for t in range(TT):
                    dve.wait_ge(v_step, a[t])
                    stand()
                    c.append(step(dve.max(vals[:, t, 8:16], rest[:, t, :])))
                for t in range(TT):
                    dve.wait_ge(v_step, c[t])
                    stand()
                    z = step(dve.max_index(idx[:, t, 8:16], vals[:, t, 8:16], rest[:, t, :]))
                dve.wait_ge(v_step, z)

            SV, SI = [SV0, SV1], [SI0, SI1]

            def keys(n, u):
                dve.wait_ge(sc_rdy, n + 1)
                top16(lambda t: A[1 + u][:, P * t:P * t + P], S2, SV[u], SI[u], n, sc_use)
                step(dve.tensor_copy(SIF[:, :, ds(n, 1), :].rearrange("p t o k -> p t (o k)"), SI[u][:, :, :]))

            def candidates(h):
                for t in range(TT):
                    z = step(dve.tensor_tensor(CD[:, t, :].rearrange("p (a b) -> p a b", a=TOPK),
                                               SV0[:, t, :].unsqueeze(2).to_broadcast((P, TOPK, TOPK)),
                                               SV1[:, t, :].unsqueeze(1).to_broadcast((P, TOPK, TOPK)), ALU.add))
                dve.wait_ge(v_step, z)
                top16(lambda t: CD[:, t, :], C2, CV, CI, h)
                step(dve.tensor_copy(TV[:, :, ds(h, 1), :].rearrange("p t o k -> p t (o k)"), CV[:, :, :]))
                step(dve.tensor_copy(TP[:, :, ds(h, 1), :].rearrange("p t o k -> p t (o k)"), CI[:, :, :]))

            query(0, 0, True)
            query(1, 1, True)
            with dve.Fori(0, 7) as i:
                loop(i, 2 * 21 + 26)
                keys(2 * i, 0)
                query(2 * i + 2, 0, False)
                keys(2 * i + 1, 1)
                candidates(i)
                query(2 * i + 3, 1, False)
                done(7)
            keys(14, 0)
            keys(15, 1)
            candidates(7)
            dve.wait_ge(v_step, here())
            step(dve.tensor_tensor(GA[:, :, :].rearrange("p t (h k) -> p (t h) k", k=TOPK),
                                   TV[:, :, :, :].rearrange("p t h k -> p (t h) k"),
                                   TV[:, :, :, 0:1].rearrange("p t h k -> p (t h) k").to_broadcast((P, TT * PH, TOPK)),
                                   ALU.subtract))
            dve.wait_ge(v_step, here())
            dve.sem_inc(sm_rdy, 1)
            pos = TP[:, :, :, :].rearrange("p t h k -> p (t h k)")
            bits = CU[:, :, :, :].rearrange("p t h k -> p (t h k)")
            for op, c, dst in ((ALU.logical_shift_right, 4, TA), (ALU.bitwise_and, 15, TB)):
                link(dve.tensor_scalar(bits, pos, c, None, op))
                link(dve.tensor_copy(dst[:, :, :].rearrange("p t k -> p (t k)"), bits))
            dve.wait_ge(sm_exp, 1)
            ga3 = GA[:, :, :].rearrange("p t (h k) -> p (t h) k", k=TOPK)
            link(dve.tensor_reduce(smx[:, :], ga3, AX.X, ALU.add))
            link(dve.reciprocal(smx[:, :], smx[:, :]))
            link(dve.tensor_tensor(ga3, ga3, smx[:, :].unsqueeze(2).to_broadcast((P, TT * PH, TOPK)), ALU.mult))

            def look(t, posf, half, dst):
                eq3 = EQ[:, :].rearrange("p (k a) -> p k a", a=TOPK)
                yield dve.tensor_tensor(eq3, posf[:, ds(t, 1), :].rearrange("p o k -> p (o k)").unsqueeze(2)
                                        .to_broadcast((P, P, TOPK)),
                                        iota[:, 0:TOPK].unsqueeze(1).to_broadcast((P, P, TOPK)), ALU.is_equal)
                eq4 = EQ[:, :].rearrange("p (h k a) -> p h k a", h=PH, a=TOPK)
                si = SIF[:, ds(t, 1), half::2, :].rearrange("p o h a -> p (o h) a").unsqueeze(2).to_broadcast((P, PH, TOPK, TOPK))
                yield dve.tensor_tensor(eq4, eq4, si, ALU.mult)
                yield dve.tensor_reduce(dst[:, ds(t, 1), :].rearrange("p o k -> p (o k)"), eq3, AX.X, ALU.add)

            with dve.Fori(0, Z_LOOK // 4) as t:
                loop(t, 6)
                parts = list(range(4))
                li, lj = look(t, TA, 0, EI), look(t, TB, 1, EJ)
                for u in parts:
                    for _ in range(2 if u < 3 else 0):
                        link(next(li) if chain["k"] < 3 else next(lj))
                    lo(4 * t + (Z1 + u + 2), u % 2)
                done(Z_LOOK // 4)
            dve.wait_ge(v_step, here())
            dve.sem_inc(rt_done, 1)
            dve.wait_ge(tr_rdy, 1)
            dve.tensor_copy(IT[:, :], A[0][:, :]).then_inc(tr_ev, 1)
            dve.wait_ge(tr_rdy, 2)
            dve.tensor_copy(JT[:, :], A[1][:, :]).then_inc(tr_ev, 1)
            dve.wait_ge(tr_ah, 1)
            dve.tensor_tensor(AL[:, :], A[2][:, :], AH[:, :].bitcast(F32), ALU.subtract).then_inc(tr_ev, 1)
            dve.wait_ge(tr_ev, 3)
            ahf, alf = AH[:, :].bitcast(F32), AL[:, :].bitcast(F32)
            with dve.Fori(0, Z_GATE // 2) as i:
                for u in range(2):
                    for g in range(2):
                        dve.wait_ge(g_mm, 4 * i + (0, 0, 1, 2)[2 * u + g])
                        oi, jh, jl = hot[3 * g:3 * g + 3]
                        for q in range(4):
                            tok = 16 * i + (8 * u + 4 * g + q)
                            dve.tensor_scalar(oi[:, q, :], iota[:, :], IT[:, ds(tok, 1)], None, ALU.is_equal)
                            dve.tensor_scalar(jh[:, q, :], iota[:, :], JT[:, ds(tok, 1)], ahf[:, ds(tok, 1)],
                                              ALU.is_equal, ALU.mult)
                            o = dve.tensor_scalar(jl[:, q, :], iota[:, :], JT[:, ds(tok, 1)], alf[:, ds(tok, 1)],
                                                  ALU.is_equal, ALU.mult)
                        o.then_inc(hot_rdy, 1)
                    lo(2 * i + (Z1 + Z_LOOK + u + 2), u)
            with dve.Fori(0, (NB_E - Z_LOOK - Z_GATE) // 2) as i:
                for u in range(2):
                    lo(2 * i + (Z1 + Z_LOOK + Z_GATE + u + 2), u)

            def product(par, jj, x0, ld):
                dve.wait_ge(zg_ld[par], ld)
                dve.wait_ge(gg_ld[par], ld)
                z3 = ZG[par][:, jj, :].rearrange("p (c t) -> p c t", t=CH)
                dve.tensor_tensor(z3, z3, GG[par][:, :, jj * CH:jj * CH + CH], ALU.mult).then_inc(act_rdy, 1)
                dve.wait_ge(x_hi, x0 + jj + 1)
                dve.tensor_tensor(XL[:, GJ * par + jj, 0:T], ZG[par][:, jj, :], XH[:, GJ * par + jj, 0:T].bitcast(F32),
                                  ALU.subtract).then_inc(x_lo, 1)

            for jj in range(GJ):
                product(0, jj, 80, 16)
            dve.wait_ge(o_ld, 16)
            banks = [[bk[0], bk[1]], [bk[2], A[0]]]

            def ogroup(gg, par, more, tail):
                for r in range(8):
                    if more:
                        product(1 - par, r, 16 * gg + (80 + 8 * par + 8), 16 * gg + 16 if par == 0 else 16 * gg + 32)
                    dve.wait_ge(w_used, 16 * gg + (O1 + 8 * par + r + 3))
                    dve.wait_ge(evac_v, 32 * gg + (120 + 16 * par - KT + 2 * r + 2))
                    for k in range(2):
                        dve.tensor_tensor(R2[:, 2 * r + k, :], banks[r % 2][k][:, :], R2[:, 2 * r + k, :], ALU.add
                                          ).then_inc(evac_v, 1)
                    if not (tail and r >= 6):
                        lo(16 * gg + (O1 + 8 * par + r + 2), r % 2)

            with dve.Fori(0, 7) as gg:
                ogroup(gg, 0, True, False)
                ogroup(gg, 1, True, False)
            ogroup(7, 0, True, False)
            ogroup(7, 1, False, True)
            dve.wait_ge(rt_rdy, 5)
            link(dve.reciprocal(rsB[:, :], rsB[:, :]))
            dve.wait_ge(evac_v, 120 + 2 * NB_E)
            for k in range(KT):
                dve.scalar_tensor_tensor(R2[:, k, :], R2[:, k, :], col[:, FNW, k:k + 1], rsB[:, :], ALU.mult, ALU.mult
                                         ).then_inc(out_rdy, 1)


def kernel(x, meta_tokens, norm1_w, w_in, b_in, mlstm_norm_w, w_mlstm_out, conv_w, conv_b, conv_ln_w, conv_ln_b,
           w_conv_out, b_conv_out, w_o, norm2_w, peer_w_q, peer_sub_keys, peer_u, peer_v, final_norm_w):
    import concourse.bacc as bacc
    from concourse.bass_utils import run_bass_kernel_spmd

    def c(a):
        return np.ascontiguousarray(a)

    def blocks(w):
        w = np.asarray(w)
        n = w.shape[1] // P
        return w.reshape(KT, P, n, P).transpose(2, 1, 0, 3).reshape(n, P, D)

    def columns(v):
        return np.asarray(v).reshape(-1, P).T

    x, meta_tokens, w, b = np.asarray(x), np.asarray(meta_tokens), np.asarray(w_in)[0], np.asarray(b_in)[0]
    tokens = np.concatenate([meta_tokens, x[0]], axis=0)
    QK, V_ = NH * P, NH * 2 * P
    gate0 = 2 * QK + 2 * V_
    glu0 = gate0 + 4 * NH
    br0 = glu0 + 2 * D
    order = []
    for h in range(NH):
        v0, o0 = 2 * QK + 2 * P * h, 2 * QK + V_ + 2 * P * h
        order += [P * h, QK + P * h, v0, v0 + P, o0, o0 + P]
    for k in range(KT):
        order += [glu0 + D + P * k, glu0 + P * k, br0 + P * k, br0 + D + P * k]
    w_proj = np.concatenate([blocks(w[:, s:s + P]) for s in order])
    bias_proj = np.stack([b[s:s + P] for s in order], axis=1)
    cols = np.stack([columns(v) for v in (norm1_w[0], norm2_w[0], final_norm_w, mlstm_norm_w[0], conv_b[0], conv_ln_w[0],
                                          conv_ln_b[0], b_conv_out[0], np.full(D, EPS, np.float32))], axis=1)
    u = np.asarray(peer_u)[0].reshape(KEYS, KEYS, KT, P)
    v = np.asarray(peer_v)[0].reshape(KEYS, KEYS // GJ, GJ, D // 256, 256)
    arrays = {
        "xT": c(tokens.T.reshape(KT, P, L).transpose(1, 0, 2)),
        "w_proj": c(w_proj),
        "w_gate": c(w[:, gate0:glu0].reshape(KT, P, 32).transpose(1, 0, 2)),
        "b_gate": c(b[gate0:glu0].reshape(32, 1)),
        "w_mo": c(blocks(w_mlstm_out[0])),
        "w_co": c(blocks(w_conv_out[0])),
        "w_o": c(blocks(w_o[0])),
        "w_q": c(blocks(peer_w_q[0])),
        "u_blocks": c(u.transpose(1, 3, 2, 0)).reshape(NB_E, P, D),
        "v_blocks": c(v.transpose(1, 3, 0, 2, 4)).reshape(NB_E, P, D),
        "cols": c(cols),
        "bias_proj": c(bias_proj),
        "conv_w": c(np.asarray(conv_w)[0].reshape(CW, KT, P).transpose(2, 1, 0).reshape(P, KT * CW)),
        "sub_keys": c(np.asarray(peer_sub_keys)[0].transpose(2, 0, 1)),
    }
    nc = bacc.Bacc("TRN2", target_bir_lowering=False, num_devices=1, dynamic_dma_scratch_size=4096)
    aps = {n: nc.dram_tensor(n, a.shape, F32, kind="ExternalInput").ap() for n, a in arrays.items()}
    out = nc.dram_tensor("out", (P, KT, T), F32, kind="ExternalOutput").ap()
    encoder_block(nc, *aps.values(), out)
    r = run_bass_kernel_spmd(nc, [arrays], core_ids=[0])
    y = r.results[0]["out"]
    return c(y.transpose(2, 1, 0).reshape(1, T, D))
```

```python
from contextlib import ExitStack

import numpy as np

import concourse.bass as bass
from concourse import mybir

F32 = mybir.dt.float32
F32R = mybir.dt.float32r
U32 = mybir.dt.uint32
ALU = mybir.AluOpType
ACT = mybir.ActivationFunctionType
AX = mybir.AxisListType
ds = bass.ds

P = 128
D = 2048
KT = D // P
NM = 16
T = 512
L = T + NM
HALF = L // 2
TT = T // P
NH = 8
CW = 31
KEYS = 128
PH = 8
TOPK = 16
QSCALE = float(P) ** -0.5
EPS = 1e-6
NEG = -3.0e38

NB_A1, NB_A2, NB_16, NB_E = 6 * NH, 4 * KT, 16, 128
A1, A2 = 0, NB_A1
B1 = A2 + NB_A2
B2 = B1 + NB_16
C1 = B2 + NB_16
Q1 = C1 + NB_16
Z1 = Q1 + NB_16
O1 = Z1 + NB_E
Z_LOOK, Z_GATE = 16, 64
TOK = T // Z_GATE
CH = 64
GJ = 8
NEXT_TILES = [[0, 1], [2], [3], [4], [5], [6], [7], []]

F_OFF = [0, 512, 896, 1152]
B_OFF = [0, 128, 384, 768]
P_W = 1280
OUT_V = 11
OUT_ORDER = [0, 1, 11, 2, 3, 12, 4, 5, 13, 6, 7, 14, 8, 9, 15, 10]


def encoder_block(nc, xT, w_proj, w_gate, b_gate, w_mo, w_co, w_o, w_q, u_blocks, v_blocks, cols,
                  bias_proj, conv_w, sub_keys, out):
    rows_dram = nc.dram_tensor("rows_scratch", (NH, 4, T), F32, kind="Internal").ap()
    ga_dram = nc.dram_tensor("gate_a_scratch", (KT, P, T), F32, kind="Internal").ap()
    gb_dram = nc.dram_tensor("gate_b_scratch", (KT, P, T), F32, kind="Internal").ap()
    h_dram = nc.dram_tensor("h_scratch", (P, KT * T), F32, kind="Internal").ap()
    z_dram = nc.dram_tensor("z_scratch", (NB_E, P, T), F32, kind="Internal").ap()
    g_dram = nc.dram_tensor("g_scratch", (T // CH, P, KEYS * CH), F32, kind="Internal").ap()

    at = [(nc.sbuf_base + 31) // 32 * 32]

    def place(name, shape, dt, offset=None):
        size = 4 * int(np.prod(shape[1:]))
        where = at[0] if offset is None else offset
        t = nc.alloc_sbuf_tensor_at(name, shape, dt, offset=where)
        if offset is None:
            at[0] += (size + 31) // 32 * 32
        return t

    XH = place("x_hi", [P, KT, L], F32R)
    XL = place("x_lo", [P, KT, L], F32R)
    RAW = [place(f"w_raw{s}", [P, D], F32) for s in range(2)]
    WH = [place(f"w_hi{s}", [P, D], F32R) for s in range(2)]
    WL = [place(f"w_lo{s}", [P, D], F32R) for s in range(2)]
    col = place("columns", [P, 9, KT], F32)
    N1W, N2W, FNW, MNW, CB, LNW, LNB, BCO, EPSC = range(9)
    bias = place("bias_proj", [P, NB_A1 + NB_A2], F32)
    nbias = place("neg_bias_o", [P, NB_A1], F32)
    cw = place("conv_w", [P, KT * CW], F32)
    sk = place("sub_keys", [P, 2, KEYS], F32)
    ones = place("ones", [P, P], F32)
    zer = place("zeros", [P, P], F32)
    ident = place("ident", [P, P], F32)
    iota = place("iota", [P, P], F32)
    cT = place("c_cols", [P, 2, TT, NH], F32)
    cM = place("c_meta", [NM, NH], F32)
    warm = place("table_warm_up", [P, 1], F32)
    r1 = at[0]
    R1 = place("r1", [P, KT, L], F32)
    r2 = at[0]
    R2 = place("r2", [P, KT, T], F32)
    dd = at[0]
    assert nc.sbuf_usable_end - dd >= 35000, nc.sbuf_usable_end - dd

    def lay(start, items):
        made, where = [], start
        for name, shape, dt in items:
            made.append(place(name, shape, dt, where))
            where += (4 * int(np.prod(shape[1:])) + 31) // 32 * 32
        return made, where

    (sq0, sq1, sq2, sq3, rb1, wg, bg, gsb), e = lay(dd, [("sq0", [P, L], F32), ("sq1", [P, L], F32),
                                          ("sq2", [P, L], F32), ("sq3", [P, L], F32), ("rb1", [P, L], F32),
                                          ("w_gate", [P, KT, 32], F32), ("b_gate", [32, 1], F32), ("gate_rows", [32, L], F32)])
    (gi, gf, gt, gF, gM, gz), e2 = lay(r2, [(n, [NH, 2, L], F32) for n in ("log_i", "f_pre", "g_tmp", "cum_f", "cum_max")]
                                  + [("g_zero", [NH, L], F32)])
    assert e2 <= dd
    (kT, qT, vT, V, VM, PF, PB, PM), e3 = lay(r1, [("kT", [P, L], F32), ("qT", [P, T], F32), ("vT", [P, 2, L], F32),
        ("V", [P, TT, 2 * P], F32), ("V_meta", [NM, 2 * P], F32), ("P_fwd", [P, P_W], F32), ("P_bwd", [P, P_W], F32),
        ("P_meta", [NM, T], F32)])
    assert e3 <= r2
    (rows, og, dF, dB, hh, hb), e4 = lay(dd, [("rows", [P, 4, T], F32), ("o_gate", [P, 2, T], F32), ("den_f", [P, T], F32),
        ("den_b", [P, T], F32), ("h_head", [P, 2, T], F32), ("h_back", [P, 2, T], F32)])
    (hs_sq, rs_h, SF, SB), e4 = lay(e4, [("h_sq", [P, 2, T], F32), ("rstd_h", [P, T], F32), ("p_sum_f", [P, T], F32),
        ("p_sum_b", [P, T], F32)])
    assert e3 + 4 * L <= r2
    sg_first = place("glu_sig_first", [P, L], F32, r2 - 4 * L)
    (cb, sg, st0, st1, cb_odd), e5 = lay(dd, [("glu", [P, 544], F32), ("glu_sig", [P, L], F32), ("ga_stage", [P, T], F32),
                                          ("gb_stage", [P, T], F32), ("conv_odd", [P, T], F32)])
    row = 4 * T
    side, e6 = lay(e5, [(f"side{u}", [P, T], F32) for u in range(2)])
    assert e6 <= dd + 8 * row
    rsB = place("rstd_b", [P, T], F32, dd + 8 * row)
    SQ, e6 = lay(dd + 9 * row, [(f"square{u}", [P, T], F32) for u in range(4)])
    (msum, ssum, tmpB, qry0), e6 = lay(e6, [(n, [P, T], F32) for n in ("mean_sum", "square_sum", "tmp_b", "qry0")])
    (qry1,), e7 = lay(e5, [("qry1", [P, T], F32)])
    qry = [qry0, qry1]
    (SIF, S2, CD, C2, TV, TP, TA, TB, SV0, SV1, SI0, SI1, CV, CI, CU), e8 = lay(r2, [("si_f", [P, TT, 2 * PH, TOPK], F32),
        ("s_rest", [P, TT, KEYS], F32), ("cand", [P, TT, 256], F32), ("cand_rest", [P, TT, 256], F32),
        ("top_v", [P, TT, PH, TOPK], F32), ("top_pos", [P, TT, PH, TOPK], U32), ("top_a", [P, TT, PH * TOPK], F32),
        ("top_b", [P, TT, PH * TOPK], F32), ("sv0", [P, TT, TOPK], F32), ("sv1", [P, TT, TOPK], F32),
        ("si0", [P, TT, TOPK], U32), ("si1", [P, TT, TOPK], U32), ("cand_v", [P, TT, TOPK], F32),
        ("cand_pos", [P, TT, TOPK], U32), ("pos_bits", [P, TT, PH, TOPK], U32)])
    assert e8 <= dd, (e8, dd)
    (EQ, GA, EI), e9 = lay(dd + 2 * row, [("eq", [P, P * TOPK], F32), ("ga", [P, TT, PH * TOPK], F32), ("ei", [P, TT, P], F32)])
    assert e9 <= dd + 8 * row
    (EJ, smx), e9 = lay(dd + 9 * row, [("ej", [P, TT, P], F32), ("smx", [P, TT * PH], F32)])
    (zs0, zs1, IT, JT, AH, AL), e10 = lay(dd, [("z_stage0", [P, T], F32), ("z_stage1", [P, T], F32), ("i_t", [P, T], F32),
        ("j_t", [P, T], F32), ("a_hi", [P, T], F32R), ("a_lo", [P, T], F32R)])
    zs = [zs0, zs1]
    assert e10 <= dd + 8 * row
    hot, e11 = lay(dd + 9 * row, [(f"{n}{s}", [P, 4, w], F32R) for s in range(2) for n, w in (("hot_i", P), ("hot_j", 2 * P))])
    hot_i, hot_j = hot[0::2], hot[1::2]
    (GB0, GB1), e12 = lay(r1, [("g_chunk0", [P, KEYS * CH], F32), ("g_chunk1", [P, KEYS * CH], F32)])
    GB = [GB0, GB1]
    assert e12 <= dd
    (GG0, GG1), e13 = lay(r1, [(f"g_group{s}", [P, T // CH, GJ * CH], F32) for s in range(2)])
    assert e13 <= r2
    (ZG1,), e14 = lay(dd, [("z_group1", [P, GJ, T], F32)])
    assert e14 <= dd + 8 * row
    (ZG0,), e14 = lay(dd + 9 * row, [("z_group0", [P, GJ, T], F32)])
    GG, ZG = [GG0, GG1], [ZG0, ZG1]
    for end in (e, e4, e5, e6, e7, e9, e11, e14):
        assert end <= nc.sbuf_usable_end, (end - dd, nc.sbuf_usable_end - dd)

    with ExitStack() as ctx:
        bk = [ctx.enter_context(nc.psum_tensor(f"bank{i}", [P, 512], F32)) for i in range(8)]
        A = bk[3:]
        o_bank = [[bk[0], A[0]], [bk[2], bk[1]]]

        def sem(name):
            return ctx.enter_context(nc.semaphore(name))

        w_loaded = [sem("w_loaded0"), sem("w_loaded1")]
        w_hi = sem("w_hi")
        w_lo = sem("w_lo")
        w_used = sem("w_used")
        evac_v = sem("evac_v")
        evac_a = sem("evac_a")
        x_hi = sem("x_hi_done")
        x_lo = sem("x_lo_done")
        x_free = sem("x_tile_free")
        v_step = sem("v_step")
        turns = [sem("turns_v"), sem("turns_p"), sem("turns_t")]
        const_ld = sem("const_loaded")
        x_ld = [sem(f"x_loaded{i}") for i in range(4)]
        pool_const = sem("pool_const")
        sq_rdy = sem("square_ready")
        sq_pair = sem("squares_paired")
        ss_use = sem("square_used")
        sq_zero = sem("square_sum_zero")
        mean_add = sem("mean_summed")
        ss_spread = sem("sum_on_all_partitions")
        rt_rdy = sem("root_ready")
        u_rdy = sem("u_ready")
        g_rdy = sem("gates_ready")
        g_row = sem("gate_rows_ready")
        g_split = sem("gate_rows_split")
        ga_step = sem("gate_act")
        gv = sem("gate_vec")
        c_rdy, c_ev = sem("c_transposed"), sem("c_columns_ready")
        r_st, r_ld = sem("rows_stored"), sem("rows_loaded")
        nb_rdy = sem("neg_bias_ready")
        e_rdy = sem("exponent_ready")
        e_exp = sem("exp_ready")
        e_msk = sem("mask_done")
        s_rdy = sem("s_ready")
        p_rdy = sem("p_ready")
        ps_rdy = sem("p_sums")
        vt_rdy, vt_ev = sem("v_turned"), sem("v_ready")
        pv_rdy, pv_use = sem("pv_ready"), sem("pv_used")
        ab_rdy = sem("abs_den_ready")
        h_rdy = sem("h_ready")
        hq_rdy, hp_rdy = sem("h_square_ready"), sem("h_squares_added")
        hs_rdy, hr_rdy = sem("h_sum_ready"), sem("h_root_ready")
        hs_done = sem("head_done")
        st_out = sem("gates_stored")
        cv_done = sem("conv_done")
        ln_m, ln_c = sem("ln_mean_ready"), sem("ln_centred")
        ln_n, ln_s = sem("ln_normed"), sem("silu_done")
        side_ld = [sem("side_loaded0"), sem("side_loaded1")]
        merged = sem("merged_ready")
        h_st, o_ld = sem("h_stored"), sem("h_reloaded")
        sc_rdy, sc_use = sem("scores_ready"), sem("scores_used")
        keys_top, cand_rdy = sem("top_keys_ready"), sem("candidates_ready")
        sm_rdy, sm_exp = sem("softmax_in"), sem("softmax_exp")
        rt_done = sem("routing_done")
        tr_rdy, tr_ev, tr_ah = sem("tables_turned"), sem("tables_ready"), sem("a_hi_ready")
        z_out = sem("z_scaled")
        z_st = [sem("z_stored0"), sem("z_stored1")]
        hot_rdy = sem("one_hots_ready")
        g_mm = sem("g_ready")
        g_ev = sem("g_copied")
        g_add = sem("g_added")
        g_st = [sem("g_stored0"), sem("g_stored1")]
        gg_ld = [sem("g_group_loaded0"), sem("g_group_loaded1")]
        zg_ld = [sem("z_group_loaded0"), sem("z_group_loaded1")]
        act_rdy = sem("act_ready")
        v_root = sem("final_root_ready")
        out_weighted = sem("out_weighted")
        out_rdy, out_rdy_p, out_st = sem("out_ready"), sem("out_ready_pool"), sem("out_stored")

        block = ctx.enter_context(nc.Block())
        r1f = R1[:, :, :].rearrange("p k t -> p (k t)")

        def r1tile(k):
            return r1f[:, k * T:k * T + T] if isinstance(k, int) else r1f[:, ds(k * T, T)]

        @block.sync
        def _(sp):
            def stream(src, nblocks, b0, first=0):
                with sp.Fori(0, (nblocks - first) // 2) as i:
                    for u in range(2):
                        sp.wait_ge(w_lo, b0 + first + u + 1 + 2 * i)
                        sp.dma_start(RAW[u][:, :], src[ds(2 * i + first + u, 1), :, :].rearrange("o p n -> (o p) n")
                                     ).then_inc(w_loaded[u], 16)

            for s in range(2):
                sp.sem_inc(g_st[s], 16)
            for s in range(4):
                sp.dma_start(R1[:, 4 * s:4 * s + 4, :], xT[:, 4 * s:4 * s + 4, :]).then_inc(x_ld[s], 16)
                if s == 0:
                    for dst, src in ((col, cols), (bias, bias_proj), (wg, w_gate), (bg, b_gate), (cw, conv_w), (sk, sub_keys)):
                        sp.dma_start(dst[:], src).then_inc(const_ld, 16)
            for u in range(2):
                sp.dma_start(RAW[u][:, :], w_proj[u]).then_inc(w_loaded[u], 16)
            stream(w_proj, NB_A1 + NB_A2, A1, first=2)
            stream(w_mo, NB_16, B1)
            stream(w_co, NB_16, B2)
            stream(w_o, NB_16, C1)
            stream(w_q, NB_16, Q1)
            def z_load(n):
                for u in range(2):
                    sp.wait_ge(w_lo, Z1 + u + 1 + n)
                    sp.dma_start(RAW[u][:, :], u_blocks[ds(n + u, 1), :, :].rearrange("o p n -> (o p) n")
                                 ).then_inc(w_loaded[u], 16)

            with sp.Fori(0, (Z_LOOK + 4) // 2) as i:
                z_load(2 * i)
            with sp.Fori(0, T // CH // 2) as cc:
                for half in range(2):
                    with sp.Fori(0, CH // TOK // 2) as m:
                        z_load(Z_LOOK + 4 + 16 * cc + 8 * half + 2 * m)
                    sp.wait_ge(g_add, 64 * cc + 32 * half + (32 + 4))
                    sp.dma_start(g_dram[ds(2 * cc + half, 1), :, :].rearrange("o p n -> (o p) n"), GB[half][:, :]
                                 ).then_inc(g_st[half], 16)
            for s in range(2):
                sp.wait_ge(g_st[s], 8 * (T // CH) + 16)
            sp.wait_ge(h_st, 16)
            sp.dma_start(R2[:, :, :], h_dram.rearrange("p (k t) -> p k t", k=KT)).then_inc(o_ld, 16)
            with sp.Fori(0, (NB_E - Z_LOOK - 4 - Z_GATE) // 2) as i:
                z_load(Z_LOOK + 4 + Z_GATE + 2 * i)
            stream(v_blocks, NB_E, O1)
            for k in OUT_ORDER:
                sp.wait_ge(*((out_rdy, k + 1) if k < OUT_V else (out_rdy_p, k - OUT_V + 1)))
                sp.dma_start(out[:, k, :], R2[:, k, :]).then_inc(out_st, 16)
            sp.wait_ge(out_st, 16 * KT)
            sp.wait_ge(st_out, 16 * 2 * KT)
            sp.wait_ge(r_st, 64)
            for s in range(2):
                sp.wait_ge(z_st[s], 16 * NB_E // 2)

        @block.gpsimd
        def _(pool):
            pool.memset(ones[:], 1.0).then_inc(pool_const, 1)
            pool.memset(zer[:], 0.0).then_inc(pool_const, 1)
            pool.memset(ident[:], 0.0).then_inc(pool_const, 1)
            pool.wait_ge(pool_const, 3)
            pool.affine_select(out=ident[:], in_=ident[:], compare_op=ALU.not_equal, fill=1.0, base=0,
                               pattern=[[-1, P]], channel_multiplier=1).then_inc(pool_const, 1)
            pool.iota(iota[:], pattern=[[1, P]], base=0, channel_multiplier=0,
                      allow_small_or_imprecise_dtypes=True).then_inc(pool_const, 1)
            pool.wait_ge(g_row, 2)
            for r, dst in enumerate((gi[:, 0, :], gf[:, 0, :], gi[:, 1, :], gf[:, 1, :])):
                pool.dma_start(dst, gsb[8 * r:8 * r + 8, :]).then_inc(g_split, 16)
            pool.wait_ge(gv, 7)
            pool.wait_ge(ga_step, 5)
            for r, (t, d) in enumerate(((gM, 0), (gt, 0), (gM, 1), (gt, 1))):
                pool.dma_start(rows_dram[:, r, :], t[:, d, NM:L]).then_inc(r_st, 16)
            pool.wait_ge(r_st, 64)
            pool.wait_ge(u_rdy, KT)
            pool.wait_ge(g_split, 64)
            def head_side(h):
                pool.wait_ge(pv_use, 4 * h)
                pool.dma_start(rows[:, :, :].rearrange("p a t -> p (a t)"),
                               rows_dram[ds(h, 1), :, :].rearrange("h a t -> h (a t)").to_broadcast((P, 4 * T))
                               ).then_inc(r_ld, 16)

            def square_sum(n):
                pool.wait_ge(hq_rdy, 2 * n)
                pool.sem_inc(turns[1], 1)
                pool.tensor_tensor(hs_sq[:, 0, :], hs_sq[:, 0, :], hs_sq[:, 1, :], ALU.add).then_inc(hp_rdy, 1)

            def masks(h):
                pool.wait_ge(e_exp, 3 * h + 3)
                pool.sem_inc(turns[1], 1)
                for j in range(TT):
                    f = PF[:, F_OFF[j]:F_OFF[j] + P]
                    pool.affine_select(out=f, in_=f, compare_op=ALU.is_ge, fill=0.0, base=0, pattern=[[1, P]],
                                       channel_multiplier=-1).then_inc(e_msk, 1)
                    q = PB[:, B_OFF[j] + P * j:B_OFF[j] + P * j + P]
                    pool.affine_select(out=q, in_=q, compare_op=ALU.is_ge, fill=0.0, base=0, pattern=[[-1, P]],
                                       channel_multiplier=1).then_inc(e_msk, 1)

            def tile_sums(h):
                pool.wait_ge(p_rdy, 9 * h + 9)
                pool.wait_ge(pv_rdy, 6 * h)
                pool.sem_inc(turns[1], 1)
                fw = lambda j: PF[:, F_OFF[j]:F_OFF[j] + T - P * j]
                bw = lambda j, n: PB[:, B_OFF[j]:B_OFF[j] + n]
                pool.tensor_copy(SF[:, 0:P], fw(0)[:, 0:P]).then_inc(ps_rdy, 1)
                pool.tensor_tensor(SF[:, P:T], fw(0)[:, P:T], fw(1), ALU.add).then_inc(ps_rdy, 1)
                pool.tensor_copy(SB[:, 3 * P:T], PB[:, B_OFF[3] + 3 * P:B_OFF[3] + T]).then_inc(ps_rdy, 1)
                pool.tensor_tensor(SB[:, 0:3 * P], bw(3, 3 * P), bw(2, 3 * P), ALU.add).then_inc(ps_rdy, 1)
                for n in range(1, 3):
                    pool.wait_ge(ps_rdy, 9 * h + 2 * n + 2)
                    pool.sem_inc(turns[1], 1)
                    pool.tensor_tensor(SF[:, P * (n + 1):T], SF[:, P * (n + 1):T], fw(n + 1), ALU.add).then_inc(ps_rdy, 1)
                    w = P * (3 - n)
                    pool.tensor_tensor(SB[:, 0:w], SB[:, 0:w], bw(2 - n, w), ALU.add).then_inc(ps_rdy, 1)
                pool.wait_ge(ps_rdy, 9 * h + 8)
                pool.sem_inc(turns[1], 1)
                pool.tensor_tensor(SF[0:NM, :], SF[0:NM, :], PM[:, :], ALU.add).then_inc(ps_rdy, 1)

            head_side(0)
            masks(0)
            tile_sums(0)
            with pool.Fori(1, NH) as h:
                head_side(h)
                square_sum(h)
                masks(h)
                tile_sums(h)
            square_sum(NH)
            pool.wait_ge(hs_done, 2 * NH)
            pool.memset(msum[:, :], 0.0).then_inc(mean_add, 1)
            pool.memset(ssum[:, :], 0.0).then_inc(sq_zero, 1)

            def gate_store(c):
                for g, (stage, dram) in enumerate(((st0, ga_dram), (st1, gb_dram))):
                    pool.wait_ge(evac_a, 6 * NH + 4 * c + 3 + g)
                    pool.sem_inc(turns[1], 1)
                    pool.dma_start(dram[ds(c, 1), :, :].rearrange("o p t -> (o p) t"), stage[:, :]).then_inc(st_out, 16)

            def mean_part(c):
                pool.wait_ge(cv_done, c + 1)
                pool.wait_ge(mean_add, c + 1)
                pool.sem_inc(turns[1], 1)
                pool.tensor_tensor(msum[:, :], msum[:, :], r1tile(c), ALU.add).then_inc(mean_add, 1)

            def square_part(n, k, s, spread=0):
                pool.wait_ge(sq_rdy, k + (n + 1))
                pool.wait_ge(ss_use, k + (n - spread))
                pool.sem_inc(turns[1], 1)
                pool.tensor_tensor(ssum[:, :], ssum[:, :], SQ[s][:, :], ALU.add).then_inc(ss_use, 1)

            with pool.Fori(0, KT - 1) as c:
                gate_store(c)
                mean_part(c)
            gate_store(KT - 1)
            pool.wait_ge(st_out, 32 * KT)

            def side_load(src, e0, n, u):
                pool.wait_ge(evac_v, n + (e0 - 1))
                if src is not None:
                    part = src[ds(n, 1), :, :].rearrange("o p t -> (o p) t")
                else:
                    part = xT[:, ds(n, 1), NM:L].rearrange("p o t -> p (o t)")
                pool.dma_start(side[u][:, :], part).then_inc(side_ld[u], 16)

            for n in range(3):
                side_load(ga_dram, 56, n, n % 2)
            mean_part(KT - 1)
            for n in range(3, 6):
                side_load(ga_dram, 56, n, n % 2)
            pool.wait_ge(sq_zero, 1)
            for k in range(KT):
                if k == KT // 2:
                    side_load(ga_dram, 56, 6, 0)
                square_part(KT, k, k % 4)
            side_load(ga_dram, 56, 7, 1)
            with pool.Fori(4, KT // 2) as i:
                for u in range(2):
                    side_load(ga_dram, 56, 2 * i + u, u)
            pool.wait_ge(ss_spread, 1)
            pool.memset(ssum[:, :], 0.0).then_inc(sq_zero, 1)
            with pool.Fori(0, KT // 2) as i:
                for u in range(2):
                    side_load(gb_dram, 72, 2 * i + u, u)
            for u in range(2):
                side_load(None, 88, u, u)
            pool.wait_ge(sq_zero, 2)
            with pool.Fori(1, KT // 2) as i:
                for u in range(2):
                    side_load(None, 88, 2 * i + u, u)
                    square_part(2 * KT, 2 * i + (u - 2), u)
            square_part(2 * KT, KT - 2, 0)
            pool.wait_ge(evac_v, 104)
            pool.dma_start(h_dram, r1f[:, 0:KT * T]).then_inc(h_st, 16)

            with pool.Fori(0, PH) as i:
                pool.wait_ge(keys_top, 2 * i + 2)
                pool.sem_inc(turns[1], 1)
                for t in range(TT):
                    pool.tensor_tensor(CD[:, t, :].rearrange("p (a b) -> p a b", a=TOPK),
                                       SV0[:, t, :].unsqueeze(2).to_broadcast((P, TOPK, TOPK)),
                                       SV1[:, t, :].unsqueeze(1).to_broadcast((P, TOPK, TOPK)), ALU.add).then_inc(cand_rdy, 1)

            def z_store(n):
                for u in range(2):
                    pool.wait_ge(evac_a, n + (112 + u + 1))
                    pool.dma_start(z_dram[ds(n + u, 1), :, :].rearrange("o p t -> (o p) t"), zs[u][:, :]
                                   ).then_inc(z_st[u], 16)

            def group_load(g, par):
                pool.dma_start(ZG[par][:, :, :], z_dram[ds(g * GJ, GJ), :, :].rearrange("j p t -> p j t")
                               ).then_inc(zg_ld[par], 16)
                pool.dma_start(GG[par][:, :, :], g_dram[:, :, ds(g * (GJ * CH), GJ * CH)].rearrange("c p n -> p c n")
                               ).then_inc(gg_ld[par], 16)

            early = Z_LOOK + Z_GATE + 8
            with pool.Fori(0, early // 2) as i:
                z_store(2 * i)
            for s in range(2):
                pool.wait_ge(g_st[s], 8 * (T // CH) + 16)
                pool.wait_ge(z_st[s], 8 * early)
            group_load(0, 0)
            with pool.Fori(0, (NB_E - early) // 2) as i:
                z_store(2 * i + early)
            for s in range(2):
                pool.wait_ge(z_st[s], 8 * NB_E)
            group_load(1, 1)
            with pool.Fori(1, KEYS // GJ // 2) as gg:
                for par in range(2):
                    pool.wait_ge(x_lo, 16 * gg + (80 + 8 * par - 8))
                    pool.sem_inc(turns[1], 1)
                    group_load(2 * gg + par, par)
            pool.wait_ge(x_lo, 80 + 8 * 15)
            pool.memset(ssum[:, :], 0.0).then_inc(sq_zero, 1)
            pool.wait_ge(sq_zero, 3)
            for k in range(KT - 2):
                square_part(3 * KT, k, k % 4, 1)
            pool.wait_ge(v_root, 1)
            for k in range(OUT_V, KT):
                pool.wait_ge(out_weighted, k - OUT_V + 1)
                pool.tensor_tensor(R2[:, k, :], R2[:, k, :], rsB[:, :], ALU.mult).then_inc(out_rdy_p, 1)

        @block.tensor
        def _(pe):
            def mm3(dst, whi, wlo, xhi, xlo, start, stop):
                pe.matmul(dst, whi, xhi, start=start, stop=False)
                pe.matmul(dst, whi, xlo, start=False, stop=False)
                return pe.matmul(dst, wlo, xhi, start=False, stop=stop)

            def blk(b, s, outs, waits, x0=None, free=False):
                pe.wait_ge(w_lo, b + 3)
                for k, (bank, c0, n) in enumerate(outs):
                    for ws, wv in waits[k]:
                        pe.wait_ge(ws, wv)
                    for kt in range(KT):
                        if x0 is not None and k == 0 and kt % 4 == 0:
                            pe.wait_ge(x_lo, x0 + kt + 4)
                        wcol = slice(kt * P, kt * P + P)
                        m = mm3(bank[:, 0:n], WH[s][:, wcol], WL[s][:, wcol], XH[:, kt, c0:c0 + n], XL[:, kt, c0:c0 + n],
                                kt == 0, kt == KT - 1)
                        if free and kt < KT - 1:
                            m.then_inc(x_free, 1)
                m.then_inc(w_used, 1)

            FULL = lambda a, b: [(a, 0, HALF), (b, HALF, HALF)]
            TOKS = lambda a: [(a, NM, T)]
            FLAT = lambda a: [(a, 0, T)]

            pe.sem_inc(w_used, 2)
            pe.wait_ge(pool_const, 5)
            for m2 in range(KT // 2):
                pe.wait_ge(sq_pair, m2 + 1)
                s = (sq0, sq2)[m2 % 2]
                for k in range(2):
                    pe.matmul(A[k][:, 0:HALF], ones[:], s[:, HALF * k:HALF * k + HALF], start=m2 == 0, stop=m2 == KT // 2 - 1
                              ).then_inc(ss_use, 1)
            pe.wait_ge(const_ld, 96)
            pe.wait_ge(w_lo, 3)
            for kt in range(KT):
                pe.wait_ge(u_rdy, kt + 1)
                pe.matmul(A[2][0:32, 0:HALF], wg[:, kt, :], R1[:, kt, 0:HALF], start=kt == 0, stop=kt == KT - 1)
                m = pe.matmul(A[3][0:32, 0:HALF], wg[:, kt, :], R1[:, kt, HALF:L], start=kt == 0, stop=kt == KT - 1)
                if kt == KT - 1:
                    m.then_inc(g_rdy, 1)
                pe.wait_ge(x_lo, kt + 1)
                wcol = slice(kt * P, kt * P + P)
                m = mm3(bk[0][:, :], WH[0][:, wcol], WL[0][:, wcol], XH[:, kt, NM:L], XL[:, kt, NM:L], kt == 0, kt == KT - 1)
            m.then_inc(w_used, 1)

            def c_columns():
                pe.wait_ge(gv, 7)
                for d in range(2):
                    for j in range(TT):
                        pe.transpose(A[4][:, (TT * d + j) * NH:(TT * d + j + 1) * NH],
                                     gi[:, d, NM + P * j:NM + P * j + P], ident[0:NH, 0:NH])
                pe.transpose(A[4][0:NM, 8 * NH:9 * NH], gi[:, 0, 0:NM], ident[0:NH, 0:NH]).then_inc(c_rdy, 1)

            def head_sum(n):
                pe.wait_ge(hp_rdy, n)
                pe.wait_ge(ab_rdy, 2 * n)
                pe.matmul(A[2][:, :], ones[:], hs_sq[:, 0, :], start=True, stop=True).then_inc(hs_rdy, 1)

            def head(h, first):
                b = 6 * h
                if not first:
                    blk(b, 0, TOKS(bk[0]), [[(evac_a, 6 * h)]])
                blk(b + 1, 1, FULL(bk[1], bk[2]), [[], []])
                if not first:
                    head_sum(h)
                blk(b + 2, 0, FULL(bk[0], bk[1]), [[(evac_v, 3 * h + 1)], [(evac_v, 3 * h + 2)]])
                if first:
                    c_columns()
                pe.wait_ge(evac_v, 3 * h + 3)
                pe.wait_ge(pv_use, 4 * h)
                pe.wait_ge(hr_rdy, h)
                for j in range(TT):
                    pe.matmul(A[j][:, :], kT[:, NM + P * j:NM + P * j + P], qT[:, :], start=True, stop=True).then_inc(s_rdy, 1)
                if first:
                    pe.wait_ge(c_ev, 2)
                pe.matmul(A[4][0:NM, :], kT[:, 0:NM], qT[:, :], start=True, stop=True).then_inc(s_rdy, 1)
                blk(b + 3, 1, FULL(bk[2], bk[0]), [[(evac_v, 3 * h + 3)], [(evac_a, 6 * h + 1)]])
                blk(b + 4, 0, TOKS(bk[1]), [[(evac_a, 6 * h + 2)]])
                pe.wait_ge(evac_a, 6 * h + 4)
                pe.wait_ge(p_rdy, 9 * h + 9)
                for v in range(2):
                    for j in range(TT):
                        m = pe.transpose(A[v][:, P * j:P * j + P], vT[:, v, NM + P * j:NM + P * j + P], ident[:])
                    m.then_inc(vt_rdy, 1)
                for v in range(2):
                    m = pe.transpose(A[2][0:NM, P * v:P * v + P], vT[:, v, 0:NM], ident[:])
                m.then_inc(vt_rdy, 1)
                blk(b + 5, 1, TOKS(bk[2]), [[(evac_a, 6 * h + 3)]])
                pe.wait_ge(vt_ev, 3 * h + 3)
                pe.wait_ge(ps_rdy, 9 * h + 9)
                pe.matmul(A[2][:, :], ones[:], SF[:, :], start=True, stop=True).then_inc(pv_rdy, 1)
                for v in range(2):
                    pe.matmul(A[3 + v][:, :], VM[:, P * v:P * v + P], PM[:, :], start=True, stop=False)
                    for j in range(TT):
                        m = pe.matmul(A[3 + v][:, P * j:T], V[:, j, P * v:P * v + P], PF[:, F_OFF[j]:F_OFF[j] + T - P * j],
                                      start=False, stop=j == TT - 1)
                    m.then_inc(pv_rdy, 1)
                pe.wait_ge(ab_rdy, 2 * h + 1)
                pe.matmul(A[2][:, :], ones[:], SB[:, :], start=True, stop=True).then_inc(pv_rdy, 1)
                for v in range(2):
                    for j in reversed(range(TT)):
                        m = pe.matmul(A[v][:, 0:P * j + P], V[:, j, P * v:P * v + P], PB[:, B_OFF[j]:B_OFF[j] + P * j + P],
                                      start=j == TT - 1, stop=j == 0)
                    m.then_inc(pv_rdy, 1)

            head(0, True)
            with pe.Fori(1, NH) as h:
                head(h, False)

            pe.wait_ge(evac_v, 3 * NH)
            def channel(c, first=False, last=False):
                b = A2 + 4 * c
                blk(b, 0, FULL(bk[0], bk[1]), [[(evac_v, 24 + 2 * c)], [(evac_a, 48 + 4 * c - 1)]])
                if first:
                    head_sum(NH)
                blk(b + 1, 1, FULL(bk[2], bk[0]), [[(evac_a, 48 + 4 * c)], [(evac_a, 48 + 4 * c + 1)]])
                blk(b + 2, 0, TOKS(bk[1]), [[(evac_a, 48 + 4 * c + 2)]])
                blk(b + 3, 1, TOKS(bk[2]), [[(evac_v, 24 + 2 * c + 1)]], free=last)

            channel(0, True)
            with pe.Fori(1, KT - 1) as c:
                channel(c)
            channel(KT - 1, last=True)

            def one(b0, e0, n, u, x0=None, free=False):
                blk(b0 + n, u, FLAT(bk[u]), [[(evac_v, e0 - 1 + n)]], x0, free)

            def pair(b0, e0, n, x0=None, free=False):
                one(b0, e0, n, 0, x0)
                one(b0, e0, n + 1, 1, free=free)

            pe.wait_ge(evac_a, 111)
            pair(B1, 56, 0, 16)
            one(B1, 56, 2, 0)
            pe.wait_ge(mean_add, KT + 1)
            pe.matmul(A[0][:, :], ones[:], msum[:, :], start=True, stop=True).then_inc(ln_m, 1)
            one(B1, 56, 3, 1)
            with pe.Fori(2, 4) as i:
                pair(B1, 56, 2 * i)
            pe.wait_ge(ss_use, 2 * KT)
            pe.matmul(A[1][:, :], ones[:], ssum[:, :], start=True, stop=True).then_inc(ss_spread, 1)
            with pe.Fori(4, 7) as i:
                pair(B1, 56, 2 * i)
            pair(B1, 56, 14, free=True)
            for b0, e0, x0 in ((B2, 72, 32), (C1, 88, 48)):
                pair(b0, e0, 0, x0)
                with pe.Fori(1, 7) as i:
                    pair(b0, e0, 2 * i)
                pair(b0, e0, 14, free=True)

            def scores(n, u):
                pe.wait_ge(evac_v, n + 105)
                if not (isinstance(n, int) and n < 2):
                    pe.wait_ge(sc_use, n - 1)
                for t in range(TT):
                    m = pe.matmul(A[1 + u][:, P * t:P * t + P], qry[u][:, P * t:P * t + P], sk[:, u, :],
                                  start=t == 0, stop=t == TT - 1, skip_group_check=True)
                m.then_inc(sc_rdy, 1)

            one(Q1, 104, 0, 0, 64)
            pe.wait_ge(ss_use, 3 * KT - 1)
            pe.matmul(A[0][:, :], ones[:], ssum[:, :], start=True, stop=False)
            pe.wait_ge(sq_rdy, 3 * KT)
            pe.matmul(A[0][:, :], ones[:], SQ[1][:, :], start=False, stop=True).then_inc(ss_spread, 1)
            one(Q1, 104, 1, 1)
            scores(0, 0)
            one(Q1, 104, 2, 0)
            scores(1, 1)
            one(Q1, 104, 3, 1)
            scores(2, 0)
            with pe.Fori(2, 8) as i:
                one(Q1, 104, 2 * i, 0)
                scores(2 * i - 1, 1)
                one(Q1, 104, 2 * i + 1, 1)
                scores(2 * i, 0)

            def zone(n, u, free=False):
                blk(Z1 + n, u, FLAT(bk[u]), [[(z_out, n - 1)]], free=free)

            blk(Z1, 0, FLAT(bk[0]), [[(evac_v, 119)]])
            scores(15, 1)
            blk(Z1 + 1, 1, FLAT(bk[1]), [[(evac_v, 120)]])
            with pe.Fori(1, Z_LOOK // 2) as i:
                for u in range(2):
                    zone(2 * i + u, u)
            pe.wait_ge(rt_done, 1)
            for k, src in enumerate((EI, EJ, GA)):
                for t in range(TT):
                    m = pe.transpose(A[k][:, P * t:P * t + P], src[:, t, :], ident[:])
                m.then_inc(tr_rdy, 1)
            pe.sem_inc(g_mm, 2)
            with pe.Fori(0, Z_GATE // 2) as i:
                for u in range(2):
                    zone(2 * i + (Z_LOOK + u), u)
                    for g in range(2):
                        pe.wait_ge(hot_rdy, 4 * i + 2 * u + g + 1)
                        pe.wait_ge(g_add, 8 * i + (4 * u + 2 * g + 2))
                        for q in range(4):
                            m = pe.matmul(A[2 * g + q // 2][:, 2 * P * (q % 2):2 * P * (q % 2) + 2 * P],
                                          hot_i[g][:, q, :], hot_j[g][:, q, :], start=q % 2 == 0, stop=q % 2 == 1,
                                          skip_group_check=True)
                        m.then_inc(g_mm, 1)
            with pe.Fori((Z_LOOK + Z_GATE) // 2, NB_E // 2 - 1) as i:
                for u in range(2):
                    zone(2 * i + u, u)
            zone(NB_E - 2, 0)
            zone(NB_E - 1, 1, free=True)

            pe.wait_ge(z_out, NB_E - 1)
            pe.wait_ge(g_add, 4 * Z_GATE + 4)
            with pe.Fori(0, KEYS // GJ // 2) as gg:
                for par in range(2):
                    pe.wait_ge(x_lo, 80 + 8 * par + 8 + 16 * gg)
                    pe.sem_inc(turns[2], 1)
                    with pe.Fori(0, 4) as m_:
                        for u in range(2):
                            n = 16 * gg + 8 * par + 2 * m_ + u
                            pe.wait_ge(w_lo, n + (O1 + 3))
                            pe.wait_ge(evac_v, 2 * n + (120 - 2))
                            for k in range(2):
                                if (u, k) == (1, 1):
                                    pe.wait_ge(z_out, NB_E)
                                for jj in range(GJ):
                                    wcol = slice(jj * 256 + k * P, jj * 256 + k * P + P)
                                    m = mm3(o_bank[u][k][:, :], WH[u][:, wcol], WL[u][:, wcol],
                                            XH[:, GJ * par + jj, 0:T], XL[:, GJ * par + jj, 0:T], jj == 0, jj == GJ - 1)
                            m.then_inc(w_used, 1)
            pe.wait_ge(ss_use, 4 * KT - 3)
            pe.matmul(A[1][:, :], ones[:], ssum[:, :], start=True, stop=False)
            for k in range(KT - 2, KT):
                pe.wait_ge(sq_rdy, 3 * KT + k + 1)
                m = pe.matmul(A[1][:, :], ones[:], SQ[k % 4][:, :], start=False, stop=k == KT - 1)
            m.then_inc(ss_spread, 1)

        @block.scalar
        def _(act):
            def hi(n_slot, b, s):
                act.wait_ge(w_loaded[s], n_slot)
                act.wait_ge(w_used, b + 1)
                act.activation(WH[s][:, :], RAW[s][:, :], ACT.Copy).then_inc(w_hi, 1)

            def hi2(b0, n, u):
                hi(8 * n + (8 * (b0 + 2) + 16), n + (b0 + 2 + u), u)

            for kt in range(KT):
                act.wait_ge(x_ld[kt // 4], 16)
                if kt >= 4:
                    act.wait_ge(ss_use, kt // 2 * 2 - 2)
                act.activation((sq0, sq1, sq2, sq3)[kt % 4][:, :], R1[:, kt, :], ACT.Square).then_inc(sq_rdy, 1)
            act.wait_ge(const_ld, 96)
            hi(16, 0, 0)
            act.activation(warm[:, :], col[:, EPSC, 0:1], ACT.Sqrt)
            act.wait_ge(ss_use, KT)
            act.activation(rb1[:, 0:HALF], A[0][:, 0:HALF], ACT.Sqrt, bias=col[:, EPSC, 0:1], scale=1.0 / D).then_inc(rt_rdy, 1)
            act.activation(rb1[:, HALF:L], A[1][:, 0:HALF], ACT.Sqrt, bias=col[:, EPSC, 0:1], scale=1.0 / D).then_inc(rt_rdy, 1)
            for kt in range(KT):
                act.wait_ge(u_rdy, kt + 1)
                act.activation(XH[:, kt, :], R1[:, kt, :], ACT.Copy).then_inc(x_hi, 1)
                if kt == 8:
                    hi(16, 1, 1)
            def forget_gates():
                act.wait_ge(g_split, 64)
                act.activation(gt[:, :, :], gf[:, :, :], ACT.Abs).then_inc(ga_step, 1)
                act.wait_ge(ga_step, 1)
                act.activation(gt[:, :, :], gt[:, :, :], ACT.Exp, scale=-1.0).then_inc(ga_step, 1)
                act.wait_ge(ga_step, 2)
                act.activation(gt[:, :, :], gt[:, :, :], ACT.Ln, bias=1.0).then_inc(ga_step, 1)

            def floors():
                act.wait_ge(gv, 7)
                for d in range(2):
                    act.activation(gt[:, d, NM:L], gt[:, d, NM:L], ACT.Exp, scale=-1.0).then_inc(ga_step, 1)

            def head_squares(n):
                for v in range(2):
                    act.wait_ge(h_rdy, 2 * n + v - 1)
                    act.activation(hs_sq[:, v, :], hh[:, v, :], ACT.Square).then_inc(hq_rdy, 1)

            def head_root(n):
                act.wait_ge(hs_rdy, n)
                act.activation(rs_h[:, :], A[2][:, :], ACT.Sqrt, bias=col[:, EPSC, 0:1], scale=1.0 / 256).then_inc(hr_rdy, 1)

            def head(h, first):
                b = 6 * h

                def nxt(u):
                    hi2(A1 + u // 2 * 2, 6 * h, u % 2)

                act.wait_ge(w_used, b + 3)
                nxt(0)
                if first:
                    forget_gates()
                else:
                    head_squares(h)
                act.wait_ge(w_used, b + 4)
                nxt(1)
                if first:
                    floors()
                else:
                    head_root(h)

                def take_v(v, banks):
                    act.wait_ge(w_used, b + 5 + v)
                    act.wait_ge(vt_rdy, 3 * h)
                    for k in range(2):
                        act.activation(vT[:, v, HALF * k:HALF * k + HALF], banks[k][:, 0:HALF], ACT.Identity,
                                       bias=bias[:, ds(b + 2 + v, 1)]).then_inc(evac_a, 1)
                    nxt(2 + v)

                if first:
                    take_v(0, (bk[0], bk[1]))
                act.wait_ge(e_rdy, 9 * h + 9)
                act.activation(PF[:, :], PF[:, :], ACT.Exp).then_inc(e_exp, 1)
                act.activation(PB[:, :], PB[:, :], ACT.Exp).then_inc(e_exp, 1)
                act.activation(PM[:, :], PM[:, :], ACT.Exp).then_inc(e_exp, 1)
                if not first:
                    take_v(0, (bk[0], bk[1]))
                take_v(1, (bk[2], bk[0]))
                act.wait_ge(nb_rdy, 1)
                act.wait_ge(hs_done, 2 * h)
                act.wait_ge(w_used, b + 7)
                act.activation(og[:, 0, :], bk[1][:, :], ACT.Exp, scale=-1.0, bias=nbias[:, ds(b + 4, 1)]).then_inc(evac_a, 1)
                nxt(4)
                act.wait_ge(pv_rdy, 6 * h)
                for v in range(2):
                    act.wait_ge(vt_rdy, 3 * h + v + 1)
                    act.activation(V[:, :, P * v:P * v + P], A[v][:, :].rearrange("p (j q) -> p j q", j=TT), ACT.Copy
                                   ).then_inc(vt_ev, 1)
                act.wait_ge(vt_rdy, 3 * h + 3)
                act.activation(VM[:, :], A[2][0:NM, 0:2 * P], ACT.Copy).then_inc(vt_ev, 1)
                act.wait_ge(w_used, b + 8)
                act.activation(og[:, 1, :], bk[2][:, :], ACT.Exp, scale=-1.0, bias=nbias[:, ds(b + 5, 1)]).then_inc(evac_a, 1)
                act.wait_ge(pv_rdy, 6 * h + 1)
                act.wait_ge(pv_use, 4 * h)
                act.activation(dF[:, :], A[2][:, :], ACT.Abs).then_inc(ab_rdy, 1)
                nxt(5)
                act.wait_ge(pv_rdy, 6 * h + 4)
                act.activation(dB[:, :], A[2][:, :], ACT.Abs).then_inc(ab_rdy, 1)

            head(0, True)
            with act.Fori(1, NH) as h:
                head(h, False)

            def channel(c, first=False, last=False):
                b = A2 + 4 * c
                sig = sg_first if first else sg
                if first:
                    head_squares(NH)
                act.wait_ge(evac_v, 24 + 2 * c)
                act.wait_ge(w_used, b + 3)
                for k in range(2):
                    act.activation(sig[:, HALF * k:HALF * k + HALF], bk[k][:, 0:HALF], ACT.Sigmoid,
                                   bias=bias[:, ds(b, 1)]).then_inc(evac_a, 1)
                hi2(A2, 4 * c, 0)
                if first:
                    head_root(NH)
                act.wait_ge(w_used, b + 4)
                hi2(A2, 4 * c, 1)
                act.wait_ge(st_out, 32 * c)
                if first:
                    act.wait_ge(hs_done, 2 * NH)
                    act.wait_ge(pv_use, 4 * NH)
                for g, (stage, bank) in enumerate(((st0, bk[1]), (st1, bk[2]))):
                    act.wait_ge(w_used, b + 5 + g)
                    act.activation(stage[:, :], bank[:, :], ACT.Sigmoid, bias=bias[:, ds(b + 2 + g, 1)]).then_inc(evac_a, 1)
                    if last and g == 1:
                        split_last(r2t, B1)
                    hi2(A2 + 2, 4 * c, g)
                    if last and g == 0:
                        split_first(r2t, 0)

            def split_first(src, phase, ready=None, scale=None):
                for k in range(KT - 1):
                    if ready is not None:
                        act.wait_ge(ready[0], ready[1] + k)
                    act.wait_ge(x_free, phase * (KT - 1) + k + 1)
                    split_tile(src, k, scale)

            def split_last(src, b0, scale=None):
                act.wait_ge(w_used, b0 + 2)
                split_tile(src, KT - 1, scale)

            def split_tile(src, k, scale):
                if scale is None:
                    act.activation(XH[:, k, 0:T], src(k), ACT.Copy).then_inc(x_hi, 1)
                else:
                    act.activation(XH[:, k, 0:T], src(k), ACT.Identity, scale=col[:, scale, k:k + 1]).then_inc(x_hi, 1)

            r2t = lambda k: R2[:, k, :]

            channel(0, True)
            with act.Fori(1, KT - 1) as c:
                channel(c)
            channel(KT - 1, last=True)

            def follow1(b0, n, u):
                act.wait_ge(w_used, b0 + 3 + n)
                hi2(b0, n - u, u)

            def follow(b0, n):
                for u in range(2):
                    follow1(b0, n + u, u)

            follow(B1, 0)
            follow(B1, 2)
            for k in range(KT):
                act.wait_ge(ln_c, k + 1)
                if k >= 4:
                    act.wait_ge(ss_use, KT + k - 3)
                act.activation(SQ[k % 4][:, :], r1tile(k), ACT.Square).then_inc(sq_rdy, 1)
                if k == KT // 2:
                    follow1(B1, 4, 0)
            follow1(B1, 5, 1)
            follow(B1, 6)
            act.wait_ge(ss_spread, 1)
            act.activation(rsB[:, :], A[1][:, :], ACT.Sqrt, bias=col[:, EPSC, 0:1], scale=1.0 / D).then_inc(rt_rdy, 1)
            follow(B1, 8)
            for k in range(KT):
                act.wait_ge(ln_n, k + 1)
                act.activation(r1tile(k), r1tile(k), ACT.Silu, scale=col[:, LNW, k:k + 1], bias=col[:, LNB, k:k + 1]).then_inc(ln_s, 1)
                if k % 8 == 7:
                    follow(B1, 10 + k // 8 * 2)
            follow1(B1, 14, 0)
            act.wait_ge(ln_s, KT)
            split_first(r1tile, 1)
            split_last(r1tile, B2)
            follow1(B1, 15, 1)
            with act.Fori(0, 7) as i:
                follow(B2, 2 * i)
            follow1(B2, 14, 0)
            split_first(r2t, 2, (merged, 1))
            act.wait_ge(merged, KT)
            split_last(r2t, C1)
            follow1(B2, 15, 1)

            def h_square(n, u):
                act.wait_ge(evac_v, 88 + 1 + n)
                act.wait_ge(ss_use, 31 + n)
                act.activation(SQ[u][:, :], r1tile(n), ACT.Square).then_inc(sq_rdy, 1)

            with act.Fori(0, 7) as i:
                for u in range(2):
                    h_square(2 * i + u, u)
                    hi2(C1, 2 * i, u)
            h_square(14, 0)
            hi2(C1, 14, 0)
            split_first(r1tile, 3, None, N2W)
            act.wait_ge(evac_v, 88 + KT)
            split_last(r1tile, Q1, N2W)
            h_square(15, 1)
            hi2(C1, 14, 1)
            act.wait_ge(ss_spread, 2)
            act.activation(rsB[:, :], A[0][:, :], ACT.Sqrt, bias=col[:, EPSC, 0:1], scale=1.0 / D).then_inc(rt_rdy, 1)
            with act.Fori(0, 8) as i:
                follow(Q1, 2 * i)
            def gelu(n, u):
                hi2(Z1, n - u, u)
                act.wait_ge(z_out, n + 1)
                act.activation(zs[u][:, :], zs[u][:, :], ACT.Gelu_apprx_tanh).then_inc(evac_a, 1)

            gelu(0, 0)
            gelu(1, 1)
            gelu(2, 0)
            act.wait_ge(sm_rdy, 1)
            act.activation(GA[:, :, :], GA[:, :, :], ACT.Exp).then_inc(sm_exp, 1)
            gelu(3, 1)
            with act.Fori(2, Z_LOOK // 2) as i:
                for u in range(2):
                    gelu(2 * i + u, u)
            act.wait_ge(tr_rdy, 3)
            act.activation(AH[:, :], A[2][:, :], ACT.Copy).then_inc(tr_ah, 1)
            act.wait_ge(tr_ah, 1)
            act.wait_ge(h_st, 16)
            with act.Fori(0, T // CH // 2) as cc:
                for half in range(2):
                    with act.Fori(0, CH // TOK // 2) as m_:
                        for u in range(2):
                            n = 16 * cc + 8 * half + 2 * m_
                            gelu(n + (Z_LOOK + u), u)
                            for g in range(2):
                                act.wait_ge(g_mm, 32 * cc + 16 * half + 4 * m_ + (2 * u + g + 3))
                                act.wait_ge(g_st[half], 16 * cc + 16)
                                dst = GB[half][:, :].rearrange("p (j t) -> p t j", t=CH)
                                for k in range(2 * g, 2 * g + 2):
                                    act.activation(dst[:, ds(16 * m_ + (8 * u + 2 * k), 2), :],
                                                   A[k][:, :].rearrange("p (t s j) -> p s t j", t=2, s=2)[:, 0, :, :], ACT.Copy
                                                   ).then_inc(g_ev, 1)
            with act.Fori((Z_LOOK + Z_GATE) // 2, NB_E // 2 - 1) as i:
                for u in range(2):
                    gelu(2 * i + u, u)
            gelu(NB_E - 2, 0)

            def act_hi(par, jj, cnt, sem_, free):
                act.wait_ge(act_rdy, cnt)
                act.wait_ge(sem_, free)
                act.activation(XH[:, GJ * par + jj, 0:T], ZG[par][:, jj, :], ACT.Copy).then_inc(x_hi, 1)

            for jj in range(GJ):
                act_hi(0, jj, jj + 1, x_free, 4 * (KT - 1) + jj + 1)
            gelu(NB_E - 1, 1)

            def out_square(k):
                act.wait_ge(evac_v, 120 + 2 * NB_E - KT + k + 1)
                if k >= 4:
                    act.wait_ge(ss_use, 3 * KT + k - 4)
                act.activation(SQ[k % 4][:, :], R2[:, k, :], ACT.Square).then_inc(sq_rdy, 1)

            def ogroup(gg, par, more, tail):
                for r in range(8):
                    b = O1 + 8 * par + r
                    u = r % 2
                    if tail and r >= 1:
                        out_square(2 * r - 2)
                        out_square(2 * r - 1)
                    act.wait_ge(w_used, 16 * gg + (b + 3))
                    if not (tail and r >= 6):
                        hi2(O1 + 8 * par + r - u, 16 * gg, u)
                    for jj in NEXT_TILES[r] if more else []:
                        act_hi(1 - par, jj, 16 * gg + (8 * par + 8 + jj + 1), w_used, 16 * gg + (O1 + 8 * par + 2))
                    if tail and r == 0:
                        act.wait_ge(x_lo, 80 + 8 * 15)

            with act.Fori(0, 7) as gg:
                ogroup(gg, 0, True, False)
                ogroup(gg, 1, True, False)
            ogroup(7, 0, True, False)
            ogroup(7, 1, False, True)
            out_square(KT - 2)
            out_square(KT - 1)
            act.wait_ge(ss_spread, 3)
            act.activation(rsB[:, :], A[1][:, :], ACT.Sqrt, bias=col[:, EPSC, 0:1], scale=1.0 / D).then_inc(rt_rdy, 1)
            act.wait_ge(sq_rdy, 4 * KT)
            for k in range(OUT_V, KT):
                act.activation(R2[:, k, :], R2[:, k, :], ACT.Identity, scale=col[:, FNW, k:k + 1]).then_inc(out_weighted, 1)

        @block.vector
        def _(dve):
            chain = {"base": 0, "i": None, "per": 0, "k": 0}

            def here():
                v = chain["base"] + chain["k"]
                return v if chain["i"] is None else chain["i"] * chain["per"] + v

            def step(ins):
                ins.then_inc(v_step, 1)
                chain["k"] += 1
                return here()

            def link(ins):
                dve.wait_ge(v_step, step(ins))

            def loop(i, per):
                chain.update(base=here(), i=i, per=per, k=0)

            def done(n):
                assert chain["k"] == chain["per"], chain
                chain.update(base=chain["base"] + n * chain["per"], i=None, k=0)

            def stand():
                dve.sem_inc(turns[0], 1)

            def lo(b, s):
                dve.wait_ge(w_hi, b + 1)
                dve.tensor_tensor(WL[s][:, :], RAW[s][:, :], WH[s][:, :].bitcast(F32), ALU.subtract).then_inc(w_lo, 1)

            dve.sem_inc(w_lo, 2)
            for m2 in range(KT // 2):
                a, b = ((sq0, sq1), (sq2, sq3))[m2 % 2]
                dve.wait_ge(sq_rdy, 2 * m2 + 2)
                dve.tensor_tensor(a[:, :], a[:, :], b[:, :], ALU.add).then_inc(sq_pair, 1)
            lo(0, 0)
            dve.wait_ge(rt_rdy, 2)
            link(dve.reciprocal(rb1[:, :], rb1[:, :]))
            dve.wait_ge(const_ld, 96)
            for kt in range(KT):
                dve.scalar_tensor_tensor(R1[:, kt, :], R1[:, kt, :], col[:, N1W, kt:kt + 1], rb1[:, :], ALU.mult, ALU.mult
                                         ).then_inc(u_rdy, 1)
                if kt >= 1:
                    dve.wait_ge(x_hi, kt)
                    dve.tensor_tensor(XL[:, kt - 1, :], R1[:, kt - 1, :], XH[:, kt - 1, :].bitcast(F32), ALU.subtract).then_inc(x_lo, 1)
            dve.wait_ge(x_hi, KT)
            dve.tensor_tensor(XL[:, KT - 1, :], R1[:, KT - 1, :], XH[:, KT - 1, :].bitcast(F32), ALU.subtract).then_inc(x_lo, 1)
            lo(1, 1)
            dve.tensor_scalar(nbias[:, :], bias[:, 0:NB_A1], -1.0, None, ALU.mult).then_inc(nb_rdy, 1)

            def take_q(h):
                dve.wait_ge(w_used, 6 * h + 3)
                dve.wait_ge(s_rdy, 5 * h)
                dve.tensor_scalar(qT[:, :], bk[0][:, :], bias[:, ds(6 * h, 1)], QSCALE, ALU.add, ALU.mult).then_inc(evac_v, 1)
                lo(6 * h + 2, 0)

            def take_k(h):
                dve.wait_ge(w_used, 6 * h + 4)
                for k in range(2):
                    dve.tensor_scalar(kT[:, HALF * k:HALF * k + HALF], bk[1 + k][:, 0:HALF], bias[:, ds(6 * h + 1, 1)], None,
                                      ALU.add).then_inc(evac_v, 1)
                lo(6 * h + 3, 1)

            dve.wait_ge(g_rdy, 1)
            dve.tensor_scalar(gsb[:, 0:HALF], A[2][0:32, 0:HALF], bg[:, 0:1], None, ALU.add).then_inc(g_row, 1)
            dve.tensor_scalar(gsb[:, HALF:L], A[3][0:32, 0:HALF], bg[:, 0:1], None, ALU.add).then_inc(g_row, 1)
            link(dve.memset(gz[:, :], 0.0))
            take_q(0)
            dve.wait_ge(g_split, 64)
            dve.wait_ge(ga_step, 3)
            dve.scalar_tensor_tensor(gf[:, :, :], gf[:, :, :], 0.0, gt[:, :, :], ALU.min, ALU.subtract).then_inc(gv, 1)
            dve.wait_ge(gv, 1)
            back = slice(L - 1, NM - 1, -1)
            dve.tensor_tensor_scan(gF[:, 0, :], gf[:, 0, :], gz[:, :], 0.0, ALU.add, ALU.add).then_inc(gv, 1)
            dve.tensor_tensor_scan(gF[:, 1, back], gf[:, 1, back], gz[:, back], 0.0, ALU.add, ALU.add).then_inc(gv, 1)
            take_k(0)
            dve.wait_ge(gv, 3)
            dve.tensor_tensor(gi[:, 0, :], gi[:, 0, :], gF[:, 0, :], ALU.subtract).then_inc(gv, 1)
            dve.tensor_tensor(gi[:, 1, NM:L], gi[:, 1, NM:L], gF[:, 1, NM:L], ALU.subtract).then_inc(gv, 1)
            dve.wait_ge(gv, 5)
            link(dve.tensor_tensor_scan(gM[:, 0, :], gi[:, 0, :], gi[:, 0, :], 0.0, ALU.max, ALU.max))
            link(dve.tensor_tensor_scan(gM[:, 1, back], gi[:, 1, back], gi[:, 1, back], 0.0, ALU.max, ALU.max))
            link(dve.tensor_tensor(gt[:, 0, NM:L], gF[:, 0, NM:L], gM[:, 0, NM:L], ALU.add))
            link(dve.tensor_tensor(gt[:, 1, NM:L], gF[:, 1, NM:L], gM[:, 1, NM:L], ALU.add))
            for d in range(2):
                dve.tensor_scalar(gM[:, d, NM:L], gM[:, d, NM:L], -1.0, None, ALU.mult).then_inc(gv, 1)
            dve.wait_ge(c_rdy, 1)
            dve.tensor_copy(cT[:, :, :, :].rearrange("p d j h -> p (d j h)"), A[4][:, 0:8 * NH]).then_inc(c_ev, 1)
            dve.tensor_copy(cM[:, :], A[4][0:NM, 8 * NH:9 * NH]).then_inc(c_ev, 1)
            dve.wait_ge(c_ev, 2)

            def quotients(n):
                dve.wait_ge(ab_rdy, 2 * n - 1)
                link(dve.tensor_tensor(dF[:, :], dF[:, :], rows[:, 1, :], ALU.max))
                link(dve.reciprocal(dF[:, :], dF[:, :]))
                dve.wait_ge(hq_rdy, 2 * n - 2)
                for v in range(2):
                    dve.wait_ge(pv_rdy, 6 * n - 4 + v)
                    dve.tensor_tensor(hh[:, v, :], A[3 + v][:, :], dF[:, :], ALU.mult).then_inc(pv_use, 1)
                dve.wait_ge(ab_rdy, 2 * n)
                link(dve.tensor_tensor(dB[:, :], dB[:, :], rows[:, 3, :], ALU.max))
                link(dve.reciprocal(dB[:, :], dB[:, :]))
                for v in range(2):
                    dve.wait_ge(pv_rdy, 6 * n - 1 + v)
                    dve.tensor_tensor(hb[:, v, :], A[v][:, :], dB[:, :], ALU.mult).then_inc(pv_use, 1)
                dve.wait_ge(pv_use, 4 * n)
                for v in range(2):
                    dve.tensor_tensor(hh[:, v, :], hh[:, v, :], hb[:, v, :], ALU.add).then_inc(h_rdy, 1)

            def head_norm(n):
                dve.wait_ge(hr_rdy, n)
                dve.wait_ge(h_rdy, 2 * n)
                link(dve.reciprocal(rs_h[:, :], rs_h[:, :]))
                for v in range(2):
                    link(dve.scalar_tensor_tensor(hh[:, v, :], hh[:, v, :], col[:, MNW, ds(2 * n + (v - 2), 1)], rs_h[:, :],
                                                  ALU.mult, ALU.mult))
                for v in range(2):
                    dve.tensor_tensor(R2[:, ds(2 * n + (v - 2), 1), :].rearrange("p o t -> p (o t)"), hh[:, v, :], og[:, v, :],
                                      ALU.mult).then_inc(hs_done, 1)

            def attention(h, first=False):
                b = 6 * h
                if first:
                    lo(b + 4, 0)
                dve.wait_ge(r_ld, 16 * h + 16)
                dve.wait_ge(pv_rdy, 6 * h)
                for j in range(TT):
                    w = T - P * j
                    dve.tensor_scalar(PF[:, F_OFF[j]:F_OFF[j] + w], rows[:, 0, P * j:T], cT[:, 0, j, ds(h, 1)], 0.0,
                                      ALU.add, ALU.min).then_inc(e_rdy, 1)
                    w = P * j + P
                    dve.tensor_scalar(PB[:, B_OFF[j]:B_OFF[j] + w], rows[:, 2, 0:w], cT[:, 1, j, ds(h, 1)], 0.0,
                                      ALU.add, ALU.min).then_inc(e_rdy, 1)
                dve.tensor_scalar(PM[:, :], rows[0:NM, 0, :], cM[:, ds(h, 1)], 0.0, ALU.add, ALU.min).then_inc(e_rdy, 1)
                if not first:
                    lo(b + 4, 0)
                dve.wait_ge(e_exp, 3 * h + 3)
                dve.wait_ge(e_msk, 8 * h + 8)
                for j in range(TT):
                    dve.wait_ge(s_rdy, 5 * h + j + 1)
                    f = PF[:, F_OFF[j]:F_OFF[j] + T - P * j]
                    dve.tensor_tensor(f, f, A[j][:, P * j:T], ALU.mult).then_inc(p_rdy, 1)
                    g = PB[:, B_OFF[j]:B_OFF[j] + P * j + P]
                    dve.tensor_tensor(g, g, A[j][:, 0:P * j + P], ALU.mult).then_inc(p_rdy, 1)
                dve.wait_ge(s_rdy, 5 * h + 5)
                dve.tensor_tensor(PM[:, :], PM[:, :], A[4][0:NM, :], ALU.mult).then_inc(p_rdy, 1)
                lo(b + 5, 1)
                for v in range(2):
                    dve.wait_ge(evac_a, 6 * h + 5 + v)
                    link(dve.tensor_scalar(og[:, v, :], og[:, v, :], 1.0, None, ALU.add))
                    link(dve.reciprocal(og[:, v, :], og[:, v, :]))
                    lo(b + 6 + v, v)

            attention(0, True)
            with dve.Fori(1, NH) as h:
                loop(h, 11)
                chain["base"] -= 11
                quotients(h)
                take_q(h)
                take_k(h)
                head_norm(h)
                attention(h)
                done(NH)
            quotients(NH)

            CONV_STEPS = CW

            def taps(c):
                sums = (r1tile(c), cb_odd[:, :])
                at_ = []
                for k in range(CW):
                    acc, w = sums[k % 2], cw[:, ds(c * CW + k, 1)]
                    x = cb[:, 1 + k:1 + k + T]
                    if k >= 2:
                        dve.wait_ge(v_step, at_[k - 2])
                        at_.append(step(dve.scalar_tensor_tensor(acc, x, w, acc, ALU.mult, ALU.add)))
                    elif k == 1:
                        at_.append(step(dve.tensor_scalar(acc, x, w, None, ALU.mult)))
                    else:
                        at_.append(step(dve.tensor_scalar(acc, x, w, col[:, CB, ds(c, 1)], ALU.mult, ALU.add)))
                    yield
                dve.wait_ge(v_step, at_[-1])
                dve.tensor_tensor(sums[0], sums[0], sums[1], ALU.add).then_inc(cv_done, 1)
                yield

            def some(g, n):
                for _ in range(n):
                    next(g)

            def conv_tile(c, first=False, last=False):
                b = A2 + 4 * c
                sig = sg_first if first else sg
                lo(b + 2, 0)
                if first:
                    head_norm(NH)
                    dve.wait_ge(hs_done, 2 * NH)
                    link(dve.memset(cb[:, L:], 0.0))
                dve.wait_ge(w_used, b + 4)
                dve.wait_ge(evac_a, 4 * c + (48 + 2))
                dve.wait_ge(cv_done, c)
                for k, bank in enumerate((bk[2], bk[0])):
                    dve.scalar_tensor_tensor(cb[:, HALF * k:HALF * k + HALF], bank[:, 0:HALF], bias[:, ds(b + 1, 1)],
                                             sig[:, HALF * k:HALF * k + HALF], ALU.add, ALU.mult).then_inc(evac_v, 1)
                lo(b + 3, 1)
                dve.wait_ge(evac_v, 2 * c + 26)
                g = taps(c)
                some(g, 9)
                lo(b + 4, 0)
                if not last:
                    some(g, 11)
                    lo(b + 5, 1)
                    some(g, CW + 1 - 20)
                return g

            conv_tile(0, True)
            with dve.Fori(1, KT - 1) as c:
                loop(c, CONV_STEPS)
                chain["base"] -= CONV_STEPS
                conv_tile(c)
                done(KT - 1)
            last_taps = conv_tile(KT - 1, last=True)

            def split(src, x0, tiles=range(KT), scale=None):
                for k in tiles:
                    dve.wait_ge(x_hi, x0 + k + 1)
                    h = XH[:, k, 0:T].bitcast(F32)
                    if scale is None:
                        dve.tensor_tensor(XL[:, k, 0:T], src(k), h, ALU.subtract).then_inc(x_lo, 1)
                    else:
                        dve.scalar_tensor_tensor(XL[:, k, 0:T], src(k), col[:, scale, k:k + 1], h, ALU.mult, ALU.subtract
                                                 ).then_inc(x_lo, 1)

            def r2tile(k):
                return R2[:, k, :] if isinstance(k, int) else R2[:, ds(k, 1), :].rearrange("p o t -> p (o t)")

            def b1(n, i, u):
                dve.wait_ge(w_used, n + (B1 + 3))
                dve.wait_ge(side_ld[u], 16 * i + 16)
                dve.tensor_tensor(r2tile(n), bk[u][:, :], side[u][:, :], ALU.mult).then_inc(evac_v, 1)
                lo(n + (B1 + 2), u)

            split(r2tile, 16)
            lo(B1 + 1, 1)
            some(last_taps, 11)
            b1(0, 0, 0)
            some(last_taps, CW + 1 - 20)
            b1(1, 0, 1)
            b1(2, 1, 0)
            dve.wait_ge(ln_m, 1)
            dve.wait_ge(cv_done, KT)
            for k in range(KT):
                dve.scalar_tensor_tensor(r1tile(k), A[0][:, :], -1.0 / D, r1tile(k), ALU.mult, ALU.add).then_inc(ln_c, 1)
            b1(3, 1, 1)
            with dve.Fori(2, 5) as i:
                for u in range(2):
                    b1(2 * i + u, i, u)
            dve.wait_ge(rt_rdy, 3)
            link(dve.reciprocal(rsB[:, :], rsB[:, :]))
            dve.wait_ge(ln_c, KT)
            for k in range(KT):
                dve.tensor_tensor(r1tile(k), r1tile(k), rsB[:, :], ALU.mult).then_inc(ln_n, 1)
                if k == 7:
                    for u in range(2):
                        b1(10 + u, 5, u)
            with dve.Fori(6, 7) as i:
                for u in range(2):
                    b1(2 * i + u, i, u)
            b1(14, 7, 0)
            split(r1tile, 32)
            b1(15, 7, 1)

            def b2(n, i, u):
                dve.wait_ge(w_used, n + (B2 + 3))
                dve.wait_ge(side_ld[u], 16 * i + (16 + 128))
                dve.wait_ge(merged, n)
                dve.scalar_tensor_tensor(tmpB[:, :], bk[u][:, :], col[:, BCO, ds(n, 1)], side[u][:, :],
                                         ALU.add, ALU.mult).then_inc(evac_v, 1)
                dve.wait_ge(evac_v, n + 73)
                dve.tensor_tensor(r2tile(n), r2tile(n), tmpB[:, :], ALU.add).then_inc(merged, 1)

            for u in range(2):
                b2(u, 0, u)
                lo(B2 + 2 + u, u)
            with dve.Fori(1, 7) as i:
                for u in range(2):
                    b2(2 * i + u, i, u)
                    lo(2 * i + (B2 + 2 + u), u)
            b2(14, 7, 0)
            lo(B2 + 16, 0)
            split(r2tile, 48, range(KT - 1))
            b2(15, 7, 1)
            split(r2tile, 48, [KT - 1])
            lo(B2 + 17, 1)

            def residual(n, i, u):
                dve.wait_ge(w_used, n + (C1 + 3))
                dve.wait_ge(side_ld[u], 16 * i + (16 + 256))
                dve.tensor_tensor(r1tile(n), bk[u][:, :], side[u][:, :], ALU.add).then_inc(evac_v, 1)

            with dve.Fori(0, 7) as i:
                for u in range(2):
                    residual(2 * i + u, i, u)
                    lo(2 * i + (C1 + 2 + u), u)
            residual(14, 7, 0)
            lo(C1 + 16, 0)
            split(r1tile, 64, range(KT - 1), N2W)
            residual(15, 7, 1)
            split(r1tile, 64, [KT - 1], N2W)
            lo(C1 + 17, 1)
            dve.wait_ge(rt_rdy, 4)
            link(dve.reciprocal(rsB[:, :], rsB[:, :]))

            def query(n, u, first):
                dve.wait_ge(w_used, n + (Q1 + 3))
                if not first:
                    dve.wait_ge(sc_rdy, n - 1)
                dve.tensor_tensor(qry[u][:, :], bk[u][:, :], rsB[:, :], ALU.mult).then_inc(evac_v, 1)
                lo(n + (Q1 + 2), u)

            def top16(src, rest, vals, idx, last=None):
                stand()
                a = [step(dve.max(vals[:, t, 0:8], src(t))) for t in range(TT)]
                for t in range(TT):
                    dve.wait_ge(v_step, a[t])
                    stand()
                    step(dve.max_index(idx[:, t, 0:8], vals[:, t, 0:8], src(t)))
                a = [step(dve.match_replace(rest[:, t, :], vals[:, t, 0:8], src(t), NEG)) for t in range(TT)]
                if last is not None:
                    dve.wait_ge(v_step, a[-1])
                    dve.sem_inc(last, 1)
                c = []
                for t in range(TT):
                    dve.wait_ge(v_step, a[t])
                    stand()
                    c.append(step(dve.max(vals[:, t, 8:16], rest[:, t, :])))
                for t in range(TT):
                    dve.wait_ge(v_step, c[t])
                    stand()
                    z = step(dve.max_index(idx[:, t, 8:16], vals[:, t, 8:16], rest[:, t, :]))
                dve.wait_ge(v_step, z)

            SV, SI = [SV0, SV1], [SI0, SI1]

            def keys(n, u):
                dve.wait_ge(sc_rdy, n + 1)
                top16(lambda t: A[1 + u][:, P * t:P * t + P], S2, SV[u], SI[u], sc_use)
                dve.sem_inc(keys_top, 1)
                step(dve.tensor_copy(SIF[:, :, ds(n, 1), :].rearrange("p t o k -> p t (o k)"), SI[u][:, :, :]))

            def candidates(h):
                dve.wait_ge(cand_rdy, TT * h + TT)
                top16(lambda t: CD[:, t, :], C2, CV, CI)
                step(dve.tensor_copy(TV[:, :, ds(h, 1), :].rearrange("p t o k -> p t (o k)"), CV[:, :, :]))
                step(dve.tensor_copy(TP[:, :, ds(h, 1), :].rearrange("p t o k -> p t (o k)"), CI[:, :, :]))

            query(0, 0, True)
            query(1, 1, True)
            with dve.Fori(0, 7) as i:
                loop(i, 2 * 21 + 22)
                keys(2 * i, 0)
                query(2 * i + 2, 0, False)
                keys(2 * i + 1, 1)
                query(2 * i + 3, 1, False)
                candidates(i)
                done(7)

            def z_scale(n, u, stored):
                dve.wait_ge(w_used, n + (Z1 + 3))
                if stored is not None:
                    dve.wait_ge(z_st[u], stored)
                dve.tensor_tensor(zs[u][:, :], bk[u][:, :], rsB[:, :], ALU.mult).then_inc(z_out, 1)
                lo(n + (Z1 + 2), u)

            keys(14, 0)
            z_scale(0, 0, None)
            keys(15, 1)
            z_scale(1, 1, None)
            candidates(7)
            z_scale(2, 0, 16)
            dve.wait_ge(v_step, here())
            step(dve.tensor_tensor(GA[:, :, :].rearrange("p t (h k) -> p (t h) k", k=TOPK),
                                   TV[:, :, :, :].rearrange("p t h k -> p (t h) k"),
                                   TV[:, :, :, 0:1].rearrange("p t h k -> p (t h) k").to_broadcast((P, TT * PH, TOPK)),
                                   ALU.subtract))
            dve.wait_ge(v_step, here())
            dve.sem_inc(sm_rdy, 1)
            pos = TP[:, :, :, :].rearrange("p t h k -> p (t h k)")
            bits = CU[:, :, :, :].rearrange("p t h k -> p (t h k)")
            for op, c, dst in ((ALU.logical_shift_right, 4, TA), (ALU.bitwise_and, 15, TB)):
                link(dve.tensor_scalar(bits, pos, c, None, op))
                link(dve.tensor_copy(dst[:, :, :].rearrange("p t k -> p (t k)"), bits))
            dve.wait_ge(sm_exp, 1)
            ga3 = GA[:, :, :].rearrange("p t (h k) -> p (t h) k", k=TOPK)
            link(dve.tensor_reduce(smx[:, :], ga3, AX.X, ALU.add))
            link(dve.reciprocal(smx[:, :], smx[:, :]))
            link(dve.tensor_tensor(ga3, ga3, smx[:, :].unsqueeze(2).to_broadcast((P, TT * PH, TOPK)), ALU.mult))

            def look(t, posf, half, dst):
                eq3 = EQ[:, :].rearrange("p (k a) -> p k a", a=TOPK)
                yield dve.tensor_tensor(eq3, posf[:, ds(t, 1), :].rearrange("p o k -> p (o k)").unsqueeze(2)
                                        .to_broadcast((P, P, TOPK)),
                                        iota[:, 0:TOPK].unsqueeze(1).to_broadcast((P, P, TOPK)), ALU.is_equal)
                eq4 = EQ[:, :].rearrange("p (h k a) -> p h k a", h=PH, a=TOPK)
                si = SIF[:, ds(t, 1), half::2, :].rearrange("p o h a -> p (o h) a").unsqueeze(2).to_broadcast((P, PH, TOPK, TOPK))
                yield dve.tensor_tensor(eq4, eq4, si, ALU.mult)
                yield dve.tensor_reduce(dst[:, ds(t, 1), :].rearrange("p o k -> p (o k)"), eq3, AX.X, ALU.add)

            def lookup(t):
                li, lj = look(t, TA, 0, EI), look(t, TB, 1, EJ)
                for u in range(3):
                    for part in range(2):
                        link(next(li) if 2 * u + part < 3 else next(lj))
                    z_scale(4 * t + (u + 3), (u + 1) % 2, 32 * t + (16 + (u + 1) // 2 * 16))

            with dve.Fori(0, TT - 2) as t:
                loop(t, 6)
                lookup(t)
                z_scale(4 * t + 6, 0, 32 * t + 48)
                done(TT - 2)
            lookup(TT - 2)
            for part in look(TT - 1, TA, 0, EI):
                link(part)
            z_scale(Z_LOOK - 2, 0, 8 * Z_LOOK - 16)
            for part in look(TT - 1, TB, 1, EJ):
                link(part)
            dve.wait_ge(v_step, here())
            dve.sem_inc(rt_done, 1)
            z_scale(Z_LOOK - 1, 1, 8 * Z_LOOK - 16)
            dve.wait_ge(tr_rdy, 1)
            dve.tensor_copy(IT[:, :], A[0][:, :]).then_inc(tr_ev, 1)
            dve.wait_ge(tr_rdy, 2)
            dve.tensor_copy(JT[:, :], A[1][:, :]).then_inc(tr_ev, 1)
            dve.wait_ge(tr_ah, 1)
            dve.tensor_tensor(AL[:, :], A[2][:, :], AH[:, :].bitcast(F32), ALU.subtract).then_inc(tr_ev, 1)
            dve.wait_ge(tr_ev, 3)
            ahf, alf = AH[:, :].bitcast(F32), AL[:, :].bitcast(F32)
            dve.sem_inc(g_add, 4)
            with dve.Fori(0, T // CH // 2) as cc:
                for half in range(2):
                    with dve.Fori(0, CH // TOK // 2) as m_:
                        for u in range(2):
                            n = 16 * cc + 8 * half + 2 * m_
                            for g in range(2):
                                dve.wait_ge(g_mm, 2 * n + (2 * u + g + 1))
                                dve.tensor_tensor(hot_i[g][:, :, :], iota[:, :].unsqueeze(1).to_broadcast((P, 4, P)),
                                                  IT[:, ds(TOK * n + (TOK * u + 4 * g), 4)].unsqueeze(2).to_broadcast((P, 4, P)),
                                                  ALU.is_equal)
                                for q in range(4):
                                    tok = TOK * n + (TOK * u + 4 * g + q)
                                    dve.tensor_scalar(hot_j[g][:, q, 0:P], iota[:, :], JT[:, ds(tok, 1)],
                                                      ahf[:, ds(tok, 1)], ALU.is_equal, ALU.mult)
                                    o = dve.tensor_scalar(hot_j[g][:, q, P:2 * P], iota[:, :], JT[:, ds(tok, 1)],
                                                          alf[:, ds(tok, 1)], ALU.is_equal, ALU.mult)
                                o.then_inc(hot_rdy, 1)
                            z_scale(n + (Z_LOOK + u), u, 8 * n + 8 * Z_LOOK)
                            for k in range(4):
                                dve.wait_ge(g_ev, 4 * n + (4 * u + k + 1))
                                dst = GB[half][:, :].rearrange("p (j t) -> p t j", t=CH)[:, ds(16 * m_ + (8 * u + 2 * k), 2), :]
                                dve.tensor_tensor(dst, dst, A[k][:, :].rearrange("p (t s j) -> p s t j", t=2, s=2)[:, 1, :, :],
                                                  ALU.add).then_inc(g_add, 1)
            with dve.Fori((Z_LOOK + Z_GATE) // 2, NB_E // 2 - 1) as i:
                for u in range(2):
                    z_scale(2 * i + u, u, 16 * i)

            def product(par, jj, ld):
                dve.wait_ge(zg_ld[par], ld)
                dve.wait_ge(gg_ld[par], ld)
                z3 = ZG[par][:, jj, :].rearrange("p (c t) -> p c t", t=CH)
                dve.tensor_tensor(z3, z3, GG[par][:, :, jj * CH:jj * CH + CH], ALU.mult).then_inc(act_rdy, 1)

            def product_lo(par, jj, x0):
                dve.wait_ge(x_hi, x0 + jj + 1)
                dve.tensor_tensor(XL[:, GJ * par + jj, 0:T], ZG[par][:, jj, :], XH[:, GJ * par + jj, 0:T].bitcast(F32),
                                  ALU.subtract).then_inc(x_lo, 1)

            for jj in range(GJ):
                product(0, jj, 16)
            z_scale(NB_E - 2, 0, 8 * NB_E - 16)
            for jj in range(GJ):
                product_lo(0, jj, 80)
            z_scale(NB_E - 1, 1, 8 * NB_E - 16)
            dve.wait_ge(o_ld, 16)

            def ogroup(gg, par, more, tail):
                for r in range(8):
                    dve.wait_ge(w_used, 16 * gg + (O1 + 8 * par + r + 3))
                    dve.wait_ge(evac_v, 32 * gg + (120 + 16 * par - KT + 2 * r + 2))
                    for k in range(2):
                        dve.tensor_tensor(R2[:, 2 * r + k, :], o_bank[r % 2][k][:, :], R2[:, 2 * r + k, :], ALU.add
                                          ).then_inc(evac_v, 1)
                    if not (tail and r >= 6):
                        lo(16 * gg + (O1 + 8 * par + r + 2), r % 2)
                    for jj in NEXT_TILES[r] if more else []:
                        product(1 - par, jj, 16 * gg + 16 if par == 0 else 16 * gg + 32)
                        product_lo(1 - par, jj, 16 * gg + (80 + 8 * par + 8))

            with dve.Fori(0, 7) as gg:
                ogroup(gg, 0, True, False)
                ogroup(gg, 1, True, False)
            ogroup(7, 0, True, False)
            ogroup(7, 1, False, True)
            dve.wait_ge(rt_rdy, 5)
            dve.reciprocal(rsB[:, :], rsB[:, :]).then_inc(v_root, 1)
            dve.wait_ge(v_root, 1)
            dve.wait_ge(evac_v, 120 + 2 * NB_E)
            for k in range(OUT_V):
                dve.scalar_tensor_tensor(R2[:, k, :], R2[:, k, :], col[:, FNW, k:k + 1], rsB[:, :], ALU.mult, ALU.mult
                                         ).then_inc(out_rdy, 1)


def kernel(x, meta_tokens, norm1_w, w_in, b_in, mlstm_norm_w, w_mlstm_out, conv_w, conv_b, conv_ln_w, conv_ln_b,
           w_conv_out, b_conv_out, w_o, norm2_w, peer_w_q, peer_sub_keys, peer_u, peer_v, final_norm_w):
    import concourse.bacc as bacc
    from concourse.bass_utils import run_bass_kernel_spmd

    def c(a):
        return np.ascontiguousarray(a)

    def blocks(w):
        w = np.asarray(w)
        n = w.shape[1] // P
        return w.reshape(KT, P, n, P).transpose(2, 1, 0, 3).reshape(n, P, D)

    def columns(v):
        return np.asarray(v).reshape(-1, P).T

    x, meta_tokens, w, b = np.asarray(x), np.asarray(meta_tokens), np.asarray(w_in)[0], np.asarray(b_in)[0]
    tokens = np.concatenate([meta_tokens, x[0]], axis=0)
    QK, V_ = NH * P, NH * 2 * P
    gate0 = 2 * QK + 2 * V_
    glu0 = gate0 + 4 * NH
    br0 = glu0 + 2 * D
    order = []
    for h in range(NH):
        v0, o0 = 2 * QK + 2 * P * h, 2 * QK + V_ + 2 * P * h
        order += [P * h, QK + P * h, v0, v0 + P, o0, o0 + P]
    for k in range(KT):
        order += [glu0 + D + P * k, glu0 + P * k, br0 + P * k, br0 + D + P * k]
    w_proj = np.concatenate([blocks(w[:, s:s + P]) for s in order])
    bias_proj = np.stack([b[s:s + P] for s in order], axis=1)
    cols = np.stack([columns(v) for v in (norm1_w[0], norm2_w[0], final_norm_w, mlstm_norm_w[0], conv_b[0], conv_ln_w[0],
                                          conv_ln_b[0], b_conv_out[0], np.full(D, EPS, np.float32))], axis=1)
    u = np.asarray(peer_u)[0].reshape(KEYS, KEYS, KT, P)
    v = np.asarray(peer_v)[0].reshape(KEYS, KEYS // GJ, GJ, D // 256, 256)
    arrays = {
        "xT": c(tokens.T.reshape(KT, P, L).transpose(1, 0, 2)),
        "w_proj": c(w_proj),
        "w_gate": c(w[:, gate0:glu0].reshape(KT, P, 32).transpose(1, 0, 2)),
        "b_gate": c(b[gate0:glu0].reshape(32, 1)),
        "w_mo": c(blocks(w_mlstm_out[0])),
        "w_co": c(blocks(w_conv_out[0])),
        "w_o": c(blocks(w_o[0])),
        "w_q": c(blocks(peer_w_q[0])),
        "u_blocks": c(u.transpose(1, 3, 2, 0)).reshape(NB_E, P, D),
        "v_blocks": c(v.transpose(1, 3, 0, 2, 4)).reshape(NB_E, P, D),
        "cols": c(cols),
        "bias_proj": c(bias_proj),
        "conv_w": c(np.asarray(conv_w)[0].reshape(CW, KT, P).transpose(2, 1, 0).reshape(P, KT * CW)),
        "sub_keys": c(np.asarray(peer_sub_keys)[0].transpose(2, 0, 1)),
    }
    nc = bacc.Bacc("TRN2", target_bir_lowering=False, num_devices=1, dynamic_dma_scratch_size=4096)
    aps = {n: nc.dram_tensor(n, a.shape, F32, kind="ExternalInput").ap() for n, a in arrays.items()}
    out = nc.dram_tensor("out", (P, KT, T), F32, kind="ExternalOutput").ap()
    encoder_block(nc, *aps.values(), out)
    r = run_bass_kernel_spmd(nc, [arrays], core_ids=[0])
    y = r.results[0]["out"]
    return c(y.transpose(2, 1, 0).reshape(1, T, D))
```
